# Optimizing a Trainium2 kernel written in Bass

```python
import jax, jax.numpy as jnp
from jax import lax
import numpy as np

D_MODEL = 1024
BATCH = 1
SEQ = 256
DEPTH = 2

CHUNK = 64
N_EVEN = (DEPTH + 1) // 2
N_ODD = DEPTH // 2
CONV_DIM = D_MODEL // 2
SHORT_CONV_K = 3
HGRN_WIDTH = D_MODEL // 2
HGRN_HEAD_DIM = 128
HGRN_HEADS = HGRN_WIDTH // HGRN_HEAD_DIM
IN_SPLITS = [CONV_DIM, 2 * CONV_DIM, 3 * CONV_DIM,
             3 * CONV_DIM + HGRN_WIDTH, 3 * CONV_DIM + 2 * HGRN_WIDTH,
             3 * CONV_DIM + 3 * HGRN_WIDTH]
IN_PROJ_DIM = 3 * CONV_DIM + 4 * HGRN_WIDTH
CONF_K = 31
D_FF = 2816
N_EXPERTS = 8
TOP_K = 2
D_FF_EXPERT = 3584
EPS = 1e-6

kernel_name = "hybrid_shortconv_hgrn2_conformer_moe"

def rmsnorm(x, g):
    xf = x.astype(jnp.float32)
    y = xf * lax.rsqrt(jnp.mean(xf * xf, axis=-1, keepdims=True) + EPS) * g.astype(jnp.float32)
    return y.astype(x.dtype)

def layernorm(x, g, b):
    xf = x.astype(jnp.float32)
    mu = jnp.mean(xf, axis=-1, keepdims=True)
    xc = xf - mu
    var = jnp.mean(xc * xc, axis=-1, keepdims=True)
    y = xc * lax.rsqrt(var + EPS) * g.astype(jnp.float32) + b.astype(jnp.float32)
    return y.astype(x.dtype)

def causal_depthwise_conv(x, w):
    K, C = w.shape
    return lax.conv_general_dilated(
        x, w[:, None, :].astype(x.dtype), window_strides=(1,), padding=[(K - 1, 0)],
        dimension_numbers=('NWC', 'WIO', 'NWC'), feature_group_count=C)

def hgrn2_chunkwise(q, k, v, log_f):
    Bsz, T, H, dk = q.shape
    dv = v.shape[-1]
    nc = T // CHUNK

    def to_chunks(a):
        return a.reshape(Bsz, nc, CHUNK, H, a.shape[-1]).transpose(1, 0, 3, 2, 4)

    qc, kc, vc, gc = to_chunks(q), to_chunks(k), to_chunks(v), to_chunks(log_f)
    causal = jnp.tril(jnp.ones((CHUNK, CHUNK), dtype=bool))

    def step(S, inp):
        q_, k_, v_, g_ = inp
        b = jnp.cumsum(g_, axis=2)
        diff = b[:, :, :, None, :] - b[:, :, None, :, :]
        decay = jnp.exp(jnp.where(causal[None, None, :, :, None], diff, -jnp.inf))
        scores = jnp.einsum('bhtd,bhsd,bhtsd->bhts', q_, k_, decay)
        o = (jnp.einsum('bhts,bhse->bhte', scores, v_)
             + jnp.einsum('bhtd,bhde->bhte', q_ * jnp.exp(b), S))
        b_last = b[:, :, -1:, :]
        S = (jnp.exp(b_last[:, :, 0, :])[..., None] * S
             + jnp.einsum('bhsd,bhse->bhde', k_ * jnp.exp(b_last - b), v_))
        return S, o

    S0 = jnp.zeros((Bsz, H, dk, dv), jnp.float32)
    _, o = lax.scan(step, S0, (qc, kc, vc, gc))
    return o.transpose(1, 0, 3, 2, 4).reshape(Bsz, T, H, dv)

def even_mixer(h, w_in, conv_w, lb, gnorm_w, w_out):
    Bsz, T, _ = h.shape
    f32 = jnp.float32
    proj = h @ w_in
    a_x, a_b, a_c, q, f, i, g = jnp.split(proj, IN_SPLITS, axis=-1)
    y_a = a_b * causal_depthwise_conv(a_c * a_x, conv_w)
    fg = lb + (1.0 - lb) * jax.nn.sigmoid(f.astype(f32))
    heads = lambda a: a.reshape(Bsz, T, HGRN_HEADS, HGRN_HEAD_DIM)
    o = hgrn2_chunkwise(heads(q.astype(f32)), heads(1.0 - fg), heads(i.astype(f32)), heads(jnp.log(fg)))
    o = rmsnorm(o, gnorm_w) * jax.nn.silu(heads(g.astype(f32)))
    y_b = o.reshape(Bsz, T, HGRN_WIDTH).astype(h.dtype)
    return jnp.concatenate([y_a, y_b], axis=-1) @ w_out

def conformer_conv(h, w_pw1, b_pw1, w_dw, b_dw, ln_g, ln_b, w_pw2, b_pw2):
    u = jax.nn.glu(h @ w_pw1 + b_pw1, axis=-1)
    u = causal_depthwise_conv(u, w_dw) + b_dw
    u = jax.nn.silu(layernorm(u, ln_g, ln_b))
    return u @ w_pw2 + b_pw2

def swiglu(h, w1, w3, w2):
    return (jax.nn.silu(h @ w1) * (h @ w3)) @ w2

def moe_swiglu(h, w_router, w1, w3, w2):
    Bsz, T, D = h.shape
    hf = h.reshape(Bsz * T, D)
    logits = (hf @ w_router).astype(jnp.float32)
    top_val, top_idx = lax.top_k(logits, TOP_K)
    gates = jax.nn.softmax(top_val, axis=-1)
    dense_gate = jnp.sum(jax.nn.one_hot(top_idx, N_EXPERTS, dtype=jnp.float32) * gates[..., None], axis=1)
    dense_gate = dense_gate.astype(h.dtype)
    out = jnp.zeros_like(hf)
    for e in range(N_EXPERTS):
        out = out + dense_gate[:, e:e + 1] * swiglu(hf, w1[e], w3[e], w2[e])
    return out.reshape(Bsz, T, D)

def setup_inputs(seed: int = 0) -> dict:
    key = jax.random.key(seed)
    ks = jax.random.split(key, 32)
    D = D_MODEL
    nrm = lambda k, shape, fan_in: jax.random.normal(k, shape, jnp.float32) * (fan_in ** -0.5)
    gain = lambda k, shape: 1.0 + 0.02 * jax.random.normal(k, shape, jnp.float32)
    small = lambda k, shape: 0.01 * jax.random.normal(k, shape, jnp.float32)
    return {
        'x': jax.random.normal(ks[0], (BATCH, SEQ, D), jnp.float32),
        'ev_norm_mix': gain(ks[1], (N_EVEN, D)),
        'ev_w_in': nrm(ks[2], (N_EVEN, D, IN_PROJ_DIM), D),
        'ev_conv_w': nrm(ks[3], (N_EVEN, SHORT_CONV_K, CONV_DIM), SHORT_CONV_K),
        'hgrn_lower_bounds': 0.1 * jax.random.normal(ks[4], (DEPTH + 1, HGRN_WIDTH), jnp.float32),
        'ev_gnorm': gain(ks[5], (N_EVEN, HGRN_HEAD_DIM)),
        'ev_w_out': nrm(ks[6], (N_EVEN, D, D), D),
        'ev_norm_ffn': gain(ks[7], (N_EVEN, D)),
        'ev_ffn_w1': nrm(ks[8], (N_EVEN, D, D_FF), D),
        'ev_ffn_w3': nrm(ks[9], (N_EVEN, D, D_FF), D),
        'ev_ffn_w2': nrm(ks[10], (N_EVEN, D_FF, D), D_FF),
        'od_norm_mix': gain(ks[11], (N_ODD, D)),
        'od_w_pw1': nrm(ks[12], (N_ODD, D, 2 * D), D),
        'od_b_pw1': small(ks[13], (N_ODD, 2 * D)),
        'od_w_dw': nrm(ks[14], (N_ODD, CONF_K, D), CONF_K),
        'od_b_dw': small(ks[15], (N_ODD, D)),
        'od_ln_g': gain(ks[16], (N_ODD, D)),
        'od_ln_b': small(ks[17], (N_ODD, D)),
        'od_w_pw2': nrm(ks[18], (N_ODD, D, D), D),
        'od_b_pw2': small(ks[19], (N_ODD, D)),
        'od_norm_ffn': gain(ks[20], (N_ODD, D)),
        'od_router': nrm(ks[21], (N_ODD, D, N_EXPERTS), D),
        'od_moe_w1': nrm(ks[22], (N_ODD, N_EXPERTS, D, D_FF_EXPERT), D),
        'od_moe_w3': nrm(ks[23], (N_ODD, N_EXPERTS, D, D_FF_EXPERT), D),
        'od_moe_w2': nrm(ks[24], (N_ODD, N_EXPERTS, D_FF_EXPERT, D), D_FF_EXPERT),
        'final_norm': gain(ks[25], (D,)),
    }

def reference(x, ev_norm_mix, ev_w_in, ev_conv_w, hgrn_lower_bounds, ev_gnorm, ev_w_out,
              ev_norm_ffn, ev_ffn_w1, ev_ffn_w3, ev_ffn_w2,
              od_norm_mix, od_w_pw1, od_b_pw1, od_w_dw, od_b_dw, od_ln_g, od_ln_b,
              od_w_pw2, od_b_pw2, od_norm_ffn, od_router, od_moe_w1, od_moe_w3, od_moe_w2,
              final_norm):
    lb_sched = jnp.cumsum(jax.nn.softmax(hgrn_lower_bounds.astype(jnp.float32), axis=0), axis=0)
    h = x
    for l in range(DEPTH):
        j = l // 2
        if l % 2 == 0:
            h = h + even_mixer(rmsnorm(h, ev_norm_mix[j]), ev_w_in[j], ev_conv_w[j],
                               lb_sched[l], ev_gnorm[j], ev_w_out[j])
            h = h + swiglu(rmsnorm(h, ev_norm_ffn[j]), ev_ffn_w1[j], ev_ffn_w3[j], ev_ffn_w2[j])
        else:
            h = h + conformer_conv(rmsnorm(h, od_norm_mix[j]), od_w_pw1[j], od_b_pw1[j],
                                   od_w_dw[j], od_b_dw[j], od_ln_g[j], od_ln_b[j],
                                   od_w_pw2[j], od_b_pw2[j])
            h = h + moe_swiglu(rmsnorm(h, od_norm_ffn[j]), od_router[j],
                               od_moe_w1[j], od_moe_w3[j], od_moe_w2[j])
    return rmsnorm(h, final_norm)


_drawn_inputs = setup_inputs


def setup_inputs(seed=0):
    import zlib

    import numpy as np

    out = dict(_drawn_inputs(seed))
    spreads = {}
    factors = {'ev_norm_ffn': 2.796,
     'od_b_pw1': 26.824,
     'od_b_dw': 3.247,
     'od_ln_b': 38.491,
     'od_b_pw2': 5.549,
     'od_norm_ffn': 2.941,
     'final_norm': 22.2,
     'od_ln_g': 2.863,
     'ev_gnorm': 2.939}
    for name, (base, spread) in spreads.items():
        noise = np.random.default_rng([zlib.crc32(name.encode()), seed]).standard_normal(out[name].shape)
        drawn = base * np.exp(spread * noise) if base else spread * noise
        out[name] = __import__('jax').numpy.asarray(drawn.astype(out[name].dtype))
    for name, factor in factors.items():
        out[name] = (out[name] * factor).astype(out[name].dtype)
    return out
```

```python
from contextlib import ExitStack

import numpy as np

import concourse.bass as bass
from concourse import mybir

P = 128
F32 = mybir.dt.float32
F32R = mybir.dt.float32r
U8 = mybir.dt.uint8
U32 = mybir.dt.uint32
I32 = mybir.dt.int32
ALU = mybir.AluOpType
ACT = mybir.ActivationFunctionType
AX = mybir.AxisListType

EPS = 1e-6
T = 256
TT = T // P
D = 1024
KD = D // P
CONV = 512
HEADS = 4
TAPS = 3
CHUNK = 64
CONF_K = 31
FF = 2816
FE = 3584
E = 8
SLOTS = P
PAD = CONF_K - 1

UNIT = 2048
RAW = 6
SPLIT = 3
AHEAD = 2
N_IN, N_OUT, N_UP, N_DOWN, N_PW1, N_PW2 = 14, 4, 22, 11, 8, 4
U_OUT = N_IN
U_UP = U_OUT + N_OUT
U_DOWN = U_UP + N_UP
U_PW1 = U_DOWN + N_DOWN
U_PW2 = U_PW1 + N_PW1
DENSE = U_PW2 + N_PW2
CHUNKS = FE // 512
PER_PASS = 4 * CHUNKS + FE // 256
PAIRS = FF // 256
assert PER_PASS % RAW == 0 and U_UP % RAW == 0 and RAW % SPLIT == 0 and PER_PASS % SPLIT == 0
TURNS = PER_PASS // RAW

AX0, AB0, AC0, Q0, F0, I0, G0 = (512 * i for i in range(7))
IN_COLS = [F0, F0 + 256, Q0, Q0 + 256, I0, I0 + 256, G0, G0 + 256,
           AX0, AC0, AB0, AX0 + 256, AC0 + 256, AB0 + 256]

V_BDW, V_LNG, V_LNB, V_BA, V_BB, V_LOW, V_CW, V_DW = 0, 1, 2, 3, 4, 5, 8, 11
NV = V_DW + CONF_K

LEVELS = 8
CROSS = LEVELS
RC = 2 * E + 1


def constants():
    s, t = np.arange(P)[:, None], np.arange(P)[None, :]
    flat = [np.eye(P), s < t, np.ones((P, P)), np.broadcast_to(t, (P, P))]
    masks = [s == t]
    for b in (1 << np.arange(LEVELS - 1)):
        masks.append((s // (2 * b) == t // (2 * b)) & (s // b % 2 == 0) & (t // b % 2 == 1))
    return (np.concatenate([np.asarray(m, np.float32) for m in flat], 1),
            np.concatenate([np.asarray(m, np.float32) for m in masks], 1))


def build_program(nc, x, ev_norm_mix, ev_w_in, ev_conv_w, hgrn_lower_bounds, ev_gnorm, ev_w_out,
                  ev_norm_ffn, ev_ffn_w1, ev_ffn_w3, ev_ffn_w2, od_norm_mix, od_w_pw1, od_b_pw1,
                  od_w_dw, od_b_dw, od_ln_g, od_ln_b, od_w_pw2, od_b_pw2, od_norm_ffn, od_router,
                  od_moe_w1, od_moe_w3, od_moe_w2, final_norm, const_f32, const_masks, out):
    with ExitStack() as ctx:
        def sb(name, shape, dt=F32):
            return ctx.enter_context(nc.sbuf_tensor(name, shape, dt))

        def sem(name):
            return ctx.enter_context(nc.semaphore(name))

        raw = sb("raw", [P, RAW, UNIT])
        w_hi = sb("w_hi", [P, SPLIT, UNIT], F32R)
        w_lo = sb("w_lo", [P, SPLIT, UNIT], F32R)
        xT_hi = sb("xT_hi", [P, 2 * D], F32R)
        xT_lo = sb("xT_lo", [P, 2 * D], F32R)
        act_hi = sb("act_hi", [P, FF * 2], F32R)
        act_lo = sb("act_lo", [P, FF * 2], F32R)
        sel = sb("sel", [P, TT, SLOTS], F32R)
        selT = sb("selT", [SLOTS, T], F32R)
        h = sb("h", [P, TT, D])
        xs = sb("xs", [P, TT, D])
        work = sb("work", [P, 6144])
        row = sb("row", [P, D])
        cst = sb("cst", [P, 4 * P])
        masks = sb("masks", [P, LEVELS, P], U8)
        vecT = sb("vecT", [P, KD, NV])
        router = sb("router", [P, KD, E])
        ss = sb("ss", [P, TT])
        ms = sb("ms", [P, TT])
        rstd = sb("rstd", [P, TT])
        mhalf = sb("mhalf", [P, 8])
        lowm = sb("lowm", [P, 4])
        lowe = sb("lowe", [P, 3, 4])
        lows = sb("lows", [P, 4])
        lb = sb("lb", [P, 4])
        olb = sb("olb", [P, 4])
        cross_off = sb("cross_off", [P, HEADS, 4])
        oss = sb("oss", [P, TT * HEADS])
        orstd = sb("orstd", [P, TT * HEADS])
        lnst = sb("lnst", [P, TT, 2, 6])
        lnmv = sb("lnmv", [P, TT, 2])
        lg = sb("lg", [P, TT, E])
        top = sb("top", [P, TT, 8])
        topi = sb("topi", [P, TT, 8], U32)
        topf = sb("topf", [P, TT, 2])
        gd = sb("gd", [P, TT])
        ge = sb("ge", [P, TT])
        g12 = sb("g12", [P, TT, 2])
        oh = sb("oh", [P, 2, TT, E])
        msk = sb("msk", [P, TT, E])
        rank = sb("rank", [P, TT, RC])
        gate = sb("gate", [P, TT, RC])
        counts = sb("counts", [P, E], I32)
        gate_slot = sb("gate_slot", [P, 1])

        ident, upper, ones, iota = (cst[:, P * i:P * (i + 1)] for i in range(4))
        gnorm_row = sb("gnorm_row", [P, P])

        dec = [xs[:, 0, :], xs[:, 1, :]]
        vec_rows = work[0:NV, 0:D]
        mask_rows = work[:, 2048:3072]
        k_t = work[:, 0:1024]
        bsum = work[:, 1024:2048]
        v_t = work[:, 2048:3072].rearrange("p (t c) -> p t c", t=TT)
        sc = work[:, 3072:4608].rearrange("p (b h t) -> p b h t", b=3, h=HEADS)
        keep = work[:, 3072:4096]
        ax = work[:, 4608:5120]
        upad = work[:, 5120:5636].rearrange("p (c t) -> p c t", c=2)
        gq = row[:, :].rearrange("p (t c) -> p t c", t=TT)
        yb = work[:, 0:1024].rearrange("p (t c) -> p t c", t=TT)
        osq = work[:, 1024:2048]
        up_s = [work[:, 512 * i:512 * (i + 1)] for i in range(3)]
        up_p = [work[:, 1536 + 512 * i:2048 + 512 * i] for i in range(3)]
        glu = work[:, 0:KD * (T + PAD)].rearrange("p (c t) -> p c t", c=KD)
        dwc = work[:, 2304:4352].rearrange("p (c t) -> p c t", c=KD)
        sg = [work[:, 4352:4864], work[:, 4864:5376]]
        zz = [work[:, 0:512], work[:, 512:1024]]
        xTf = work[:, 0:2048].rearrange("p (c t) -> p c t", c=KD)
        moe_s = [work[:, 0:512], work[:, 512:1024]]
        moe_p = [work[:, 1024:1536], work[:, 1536:2048]]
        selg = work[:, 2048:2304].rearrange("p (t s) -> p t s", t=TT)
        xg_hi, xg_lo = xT_hi[:, 0:D], xT_lo[:, 0:D]
        y_hi, y_lo = xT_hi[:, D:2 * D], xT_lo[:, D:2 * D]
        xs_hi = act_hi[:, FE:FE + 2 * D].rearrange("p (t c) -> p t c", t=TT)
        xs_lo = act_lo[:, FE:FE + 2 * D].rearrange("p (t c) -> p t c", t=TT)

        ps = ctx.enter_context(nc.psum_tensor("ps", [P, 8, 512], F32))

        landed = [sem(f"landed{i}") for i in range(RAW)]
        x_in = sem("x_in")
        cst_in = sem("cst_in")
        vec_in = sem("vec_in")
        row_in = sem("row_in")
        out_done = sem("out_done")
        hi_done = sem("hi_done")
        lo_done = sem("lo_done")
        unit_done = sem("unit_done")
        zeroed = sem("zeroed")
        sq_done = sem("sq_done")
        ms_ready = sem("ms_ready")
        rstd_ready = sem("rstd_ready")
        xs_ready = sem("xs_ready")
        turned = sem("turned")
        xh_done = sem("xh_done")
        xl_done = sem("xl_done")
        vec_turned = sem("vec_turned")
        low_dif = sem("low_dif")
        masks_ready = sem("masks_ready")
        low_exp = sem("low_exp")
        dve_own = sem("dve_own")
        sig_done = sem("sig_done")
        fg_ready = sem("fg_ready")
        ln_done = sem("ln_done")
        k_ready = sem("k_ready")
        q_copied = sem("q_copied")
        e_ready = sem("e_ready")
        exp_done = sem("exp_done")
        dec_ready = sem("dec_ready")
        scored = sem("scored")
        masked = sem("masked")
        cross_copied = sem("cross_copied")
        in_copied = sem("in_copied")
        ac_read = sem("ac_read")
        ab_read = sem("ab_read")
        ya_hi = sem("ya_hi")
        ya_lo = sem("ya_lo")
        g_silu = sem("g_silu")
        o_done = sem("o_done")
        o_sq = sem("o_sq")
        o_sum = sem("o_sum")
        o_ms = sem("o_ms")
        o_rstd = sem("o_rstd")
        yb_ready = sem("yb_ready")
        yb_turned = sem("yb_turned")
        yb_hi = sem("yb_hi")
        yb_lo = sem("yb_lo")
        res_added = sem("res_added")
        up_silu = sem("up_silu")
        up_mul = sem("up_mul")
        up_hi = sem("up_hi")
        up_lo = sem("up_lo")
        sg_done = sem("sg_done")
        glu_done = sem("glu_done")
        conv_step = sem("conv_step")
        conv_turned = sem("conv_turned")
        ln_var = sem("ln_var")
        ln_ms = sem("ln_ms")
        ln_rstd = sem("ln_rstd")
        ln_ready = sem("ln_ready")
        ln_turned = sem("ln_turned")
        z_silu = sem("z_silu")
        z_hi = sem("z_hi")
        z_lo = sem("z_lo")
        bias_added = sem("bias_added")
        xsh_done = sem("xsh_done")
        xsl_done = sem("xsl_done")
        logits_done = sem("logits_done")
        gd_ready = sem("gd_ready")
        ge_done = sem("ge_done")
        mask_ready = sem("mask_ready")
        rank_done = sem("rank_done")
        routed = sem("routed")
        sel_ready = sem("sel_ready")
        gathered = sem("gathered")
        gath_hi = sem("gath_hi")
        gath_lo = sem("gath_lo")
        moe_ready = sem("moe_ready")
        silu_done = sem("silu_done")
        mul_done = sem("mul_done")
        act_turned = sem("act_turned")
        ah_done = sem("ah_done")
        al_done = sem("al_done")
        selg_turned = sem("selg_turned")
        selT_done = sem("selT_done")
        yh_done = sem("yh_done")
        yl_done = sem("yl_done")
        comb_done = sem("comb_done")
        comb_added = sem("comb_added")
        fin_ready = sem("fin_ready")

        w_in, w_out = ev_w_in[0], ev_w_out[0]
        w1, w3, w2 = ev_ffn_w1[0], ev_ffn_w3[0], ev_ffn_w2[0]
        pw1, pw2 = od_w_pw1[0], od_w_pw2[0]

        def hi_unit(k):
            return w_hi[:, k % SPLIT, :]

        def lo_unit(k):
            return w_lo[:, k % SPLIT, :]

        def split_hi(act, k, turn=0):
            act.wait_ge(landed[k % RAW], 16 * turn + 16 * (k // RAW + 1))
            if k >= SPLIT:
                act.wait_ge(unit_done, RAW * turn + k - SPLIT + 1)
            act.activation(hi_unit(k), raw[:, k % RAW, :], ACT.Copy).then_inc(hi_done, 1)

        def split_lo(dve, k, turn=0):
            dve.wait_ge(hi_done, RAW * turn + k + 1)
            dve.tensor_tensor(lo_unit(k), raw[:, k % RAW, :], hi_unit(k).bitcast(F32),
                              ALU.subtract).then_inc(lo_done, 1)

        def load(sp, k, src, turn=0):
            if k >= RAW:
                sp.wait_ge(lo_done, RAW * turn + k - RAW + 1)
            sp.dma_start(raw[:, k % RAW, :].rearrange("p (r n) -> p r n", r=src.shape[1]),
                         src).then_inc(landed[k % RAW], 16)

        def cols(w, n0, n):
            return w[:, bass.ds(n0, n)].rearrange("(k p) n -> p k n", p=P)

        def rows(w, k0, k):
            return w[k0 * P:(k0 + k) * P, :].rearrange("(k p) n -> p k n", p=P)

        block = ctx.enter_context(nc.Block())

        @block.sync
        def _(sp):
            for t in range(TT):
                sp.dma_start(h[:, t, :], x[0, t * P:(t + 1) * P, :]).then_inc(x_in, 16)
            for k in range(N_IN):
                load(sp, k, cols(w_in, IN_COLS[k], 256))
            for j in range(N_OUT):
                load(sp, U_OUT + j, rows(w_out, 2 * j, 2))
            with sp.Fori(0, PAIRS // 3) as i:
                for m in range(3):
                    load(sp, U_UP + 2 * m, cols(w1, i * 768 + 256 * m, 256), i)
                    load(sp, U_UP + 2 * m + 1, cols(w3, i * 768 + 256 * m, 256), i)
            for j in range(PAIRS // 3 * 3, PAIRS):
                load(sp, U_UP + 2 * j, cols(w1, 256 * j, 256))
                load(sp, U_UP + 2 * j + 1, cols(w3, 256 * j, 256))
            for j in range(N_DOWN):
                load(sp, U_DOWN + j, rows(w2, 2 * j, 2))
            for j in range(N_PW1 // 2):
                load(sp, U_PW1 + 2 * j, cols(pw1, 256 * j, 256))
                load(sp, U_PW1 + 2 * j + 1, cols(pw1, D + 256 * j, 256))
            for j in range(N_PW2):
                load(sp, U_PW2 + j, rows(pw2, 2 * j, 2))

            def one(w, e):
                return w[0, bass.ds(e, 1)].rearrange("a k n -> (a k) n")

            def expert_loads(e, p):
                e1, e3, e2 = one(od_moe_w1, e), one(od_moe_w3, e), one(od_moe_w2, e)
                for k in range(PER_PASS):
                    if k < 4 * CHUNKS:
                        src = (e1 if k % 4 < 2 else e3)[k % 2 * 512:k % 2 * 512 + 512, k // 4 * 512:(k // 4 + 1) * 512]
                        src = src.rearrange("(k p) n -> p k n", p=P)
                    else:
                        src = rows(e2, 2 * (k - 4 * CHUNKS), 2)
                    load(sp, DENSE + k, src, TURNS * p)

            with sp.Fori(0, E) as e:
                expert_loads(e, e)
            sp.wait_ge(routed, 1)
            passes = sp.alloc_register("sp_passes")
            sp.reg_mov(passes, E)
            with sp.Fori(0, E) as e:
                n = sp.value_load(counts[0:1, bass.ds(e, 1)])
                with sp.If(n > SLOTS):
                    expert_loads(e, sp.snap(passes))
                    sp.reg_add(passes, passes, 1)
                with sp.Else():
                    sp.nop()
                sp.nop()
            for t in range(TT):
                sp.wait_ge(fin_ready, t + 1)
                sp.dma_start(out[0, t * P:(t + 1) * P, :], xs[:, t, :]).then_inc(out_done, 16)
            sp.wait_ge(out_done, 16 * TT)

        @block.gpsimd
        def _(pool):
            def load_row(vec):
                pool.dma_start(row[:, :], vec.to_broadcast([P, D])).then_inc(row_in, 16)

            def inverse_root(n, into, src, scale, cnt, m, m_ready, r_ready):
                pool.tensor_scalar(m, src, scale, EPS, ALU.mult, ALU.add).then_inc(m_ready, 1)
                pool.wait_ge(m_ready, n)
                pool.tensor_tensor(into, m, mhalf[:, 0:cnt], ALU.pow).then_inc(r_ready, 1)

            def norm(n):
                pool.wait_ge(sq_done, 2 * (n + 1))
                if n:
                    pool.wait_ge(xs_ready, 2 * n)
                inverse_root(n + 1, rstd[:, :], ss[:, :], 1.0 / D, TT, ms[:, :], ms_ready, rstd_ready)

            load_row(ev_norm_mix[0:1, :])
            pool.memset(mhalf[:, :], -0.5).then_inc(zeroed, 1)
            pool.wait_ge(zeroed, 1)
            norm(0)
            pool.wait_ge(o_sum, TT)
            pool.tensor_scalar(osq[:, 0:8], oss[:, :], 1.0 / P, EPS, ALU.mult, ALU.add).then_inc(o_ms, 1)
            pool.wait_ge(o_ms, 1)
            pool.tensor_tensor(orstd[:, :], osq[:, 0:8], mhalf[:, :], ALU.pow).then_inc(o_rstd, 1)
            pool.wait_ge(yb_ready, 2)
            load_row(ev_norm_ffn[0:1, :])
            norm(1)
            pool.wait_ge(xs_ready, 4)
            load_row(od_norm_mix[0:1, :])
            norm(2)
            pool.wait_ge(xs_ready, 6)
            load_row(od_b_pw2[0:1, :])
            pool.wait_ge(bias_added, 2)
            load_row(od_norm_ffn[0:1, :])
            pool.wait_ge(ln_var, 1)
            pool.tensor_scalar(ms[:, :], lnmv[:, :, 1], 1.0, EPS, ALU.mult, ALU.add).then_inc(ln_ms, 1)
            pool.wait_ge(ln_ms, 1)
            pool.tensor_tensor(rstd[:, :], ms[:, :], mhalf[:, 0:TT], ALU.pow).then_inc(ln_rstd, 1)
            pool.wait_ge(ln_ready, 2)
            norm(3)
            pool.wait_ge(xs_ready, 8)
            load_row(final_norm.unsqueeze(0))
            norm(4)

        @block.scalar
        def _(act):
            act.dma_start(cst[:, :], const_f32).then_inc(cst_in, 16)
            for r, v in ((V_BDW, od_b_dw), (V_LNG, od_ln_g), (V_LNB, od_ln_b)):
                act.dma_start(vec_rows[r:r + 1, :], v[0:1, :]).then_inc(vec_in, 16)
            act.dma_start(vec_rows[V_BA:V_BA + 2, :], od_b_pw1.rearrange("a (r c) -> (a r) c", r=2)).then_inc(vec_in, 16)
            act.dma_start(vec_rows[V_DW:V_DW + CONF_K, :], od_w_dw[0]).then_inc(vec_in, 16)
            for a in range(2):
                act.dma_start(vec_rows[V_LOW:V_LOW + 3, a * CONV:(a + 1) * CONV], hgrn_lower_bounds).then_inc(vec_in, 16)
                act.dma_start(vec_rows[V_CW:V_CW + TAPS, a * CONV:(a + 1) * CONV], ev_conv_w[0]).then_inc(vec_in, 16)
            act.dma_start(mask_rows, const_masks).then_inc(cst_in, 16)
            act.dma_start(router[:, :, :], od_router[0].rearrange("(k p) e -> p k e", p=P)).then_inc(cst_in, 16)
            act.dma_start(gnorm_row[:, :], ev_gnorm[0:1, :].to_broadcast([P, P])).then_inc(cst_in, 16)

            def squares(n):
                for t in range(TT):
                    if n == 0:
                        act.wait_ge(x_in, 16 * TT)
                    act.activation(xs[:, t, :], h[:, t, :], ACT.Square,
                                   accum_out=ss[:, t:t + 1]).then_inc(sq_done, 1)

            def turned_hi(n, b0):
                for j in range(4):
                    act.wait_ge(turned, 4 * n + j + 1)
                    act.activation(xT_hi[:, 512 * j:512 * (j + 1)], ps[:, b0 + j, :], ACT.Copy).then_inc(xh_done, 1)

            def tick(k):
                if k + AHEAD < DENSE:
                    split_hi(act, k + AHEAD)

            squares(0)
            for k in range(AHEAD):
                split_hi(act, k)
            act.wait_ge(low_dif, 1)
            act.activation(lowe[:, :, :], lowe[:, :, :], ACT.Exp).then_inc(low_exp, 1)
            turned_hi(0, 4)
            for k in range(N_IN):
                tick(k)
                if k < 2:
                    act.wait_ge(unit_done, k + 1)
                    act.activation(dec[0][:, 512 * k:512 * (k + 1)], ps[:, k, :], ACT.Sigmoid).then_inc(sig_done, 1)
                if k == 2:
                    act.wait_ge(fg_ready, 1)
                    act.activation(dec[1], dec[0], ACT.Ln).then_inc(ln_done, 1)
                if k == 3:
                    act.wait_ge(k_ready, 1)
                    act.wait_ge(ln_done, 1)
                    act.wait_ge(unit_done, 4)
                    act.activation(dec[0].rearrange("p (b n) -> p b n", b=2), ps[:, 2:4, :],
                                   ACT.Copy).then_inc(q_copied, 1)
                if k == 4:
                    act.wait_ge(masks_ready, 1)
                if k in (4, 5, 6, 7):
                    act.wait_ge(unit_done, k + 1)
                    into = (v_t if k < 6 else gq)[:, :, 256 * (k % 2):256 * (k % 2 + 1)]
                    act.activation(into, ps[:, k % 2, :].rearrange("p (t c) -> p t c", t=TT),
                                   ACT.Copy).then_inc(in_copied, 1)
                if k in (8, 11):
                    act.wait_ge(unit_done, k + 1)
                    if k == 11:
                        act.wait_ge(ya_lo, 1)
                    act.activation(ax, ps[:, 0 if k == 8 else 1, :], ACT.Copy).then_inc(in_copied, 1)
                if 4 <= k <= 11:
                    level = k - 3
                    act.wait_ge(e_ready, level)
                    act.activation(dec[level % 2], dec[level % 2], ACT.Exp).then_inc(exp_done, 1)
                if k in (10, 13):
                    half = (k - 10) // 3
                    act.wait_ge(ab_read, half + 1)
                    act.activation(act_hi[:, 512 * half:512 * (half + 1)], ax, ACT.Copy).then_inc(ya_hi, 1)
                if k == 12:
                    act.wait_ge(in_copied, 4)
                    act.activation(row[:, :], row[:, :], ACT.Silu).then_inc(g_silu, 1)
                    act.wait_ge(scored, 2 * LEVELS + 1)
                    act.activation(sc[:, 1, :, :], ps[:, 4, :].rearrange("p (h t) -> p h t", h=HEADS),
                                   ACT.Copy).then_inc(cross_copied, 1)
            for j in range(N_OUT):
                tick(U_OUT + j)
                if j == 0:
                    for t in range(TT):
                        act.wait_ge(o_done, t + 1)
                        act.activation(osq[:, 512 * t:512 * (t + 1)], ps[:, 6 + t, :], ACT.Square).then_inc(o_sq, 1)
                if j == 1:
                    for b in range(2):
                        act.wait_ge(yb_turned, b + 1)
                        act.activation(act_hi[:, D + 512 * b:D + 512 * (b + 1)], ps[:, 4 + b, :],
                                       ACT.Copy).then_inc(yb_hi, 1)
            act.wait_ge(res_added, 4)
            squares(1)
            turned_hi(1, 4)

            def up_ticks(m, i=0):
                k = U_UP + 2 * m
                split_hi(act, k + AHEAD, i)
                act.wait_ge(unit_done, RAW * i + k + 1)
                act.activation(up_s[m % 3], ps[:, 2 * (m % 3), :], ACT.Silu).then_inc(up_silu, 1)
                split_hi(act, k + 1 + AHEAD, i)
                act.wait_ge(up_mul, 3 * i + m + 1)
                act.activation(act_hi[:, bass.ds(i * 1536 + 512 * m, 512)], up_p[m % 3], ACT.Copy).then_inc(up_hi, 1)

            with act.Fori(0, PAIRS // 3) as i:
                for m in range(3):
                    up_ticks(m, i)
            for m in range(PAIRS // 3 * 3, PAIRS):
                up_ticks(m)
            for j in range(N_DOWN):
                tick(U_DOWN + j)
            act.wait_ge(res_added, 8)
            squares(2)
            turned_hi(2, 0)
            for j in range(N_PW1 // 2):
                tick(U_PW1 + 2 * j)
                tick(U_PW1 + 2 * j + 1)
                act.wait_ge(unit_done, U_PW1 + 2 * j + 2)
                if j >= 2:
                    act.wait_ge(glu_done, 2 * (j - 1))
                for m in range(2):
                    c = 2 * j + m
                    act.activation(sg[j % 2][:, T * m:T * (m + 1)], ps[:, 5 + 2 * (j % 2), T * m:T * (m + 1)],
                                   ACT.Sigmoid, bias=vecT[:, c, V_BB:V_BB + 1]).then_inc(sg_done, 1)
            for j in range(4):
                act.wait_ge(ln_turned, j + 1)
                if j >= 2:
                    act.wait_ge(z_lo, j - 1)
                for m in range(2):
                    c = 2 * j + m
                    act.activation(zz[j % 2][:, T * m:T * (m + 1)], ps[:, 4 + j, T * m:T * (m + 1)], ACT.Silu,
                                   bias=vecT[:, c, V_LNB:V_LNB + 1],
                                   scale=vecT[:, c, V_LNG:V_LNG + 1]).then_inc(z_silu, 1)
                act.wait_ge(z_silu, 2 * (j + 1))
                act.activation(act_hi[:, 512 * j:512 * (j + 1)], zz[j % 2], ACT.Copy).then_inc(z_hi, 1)
            for j in range(N_PW2):
                tick(U_PW2 + j)
            act.wait_ge(res_added, 12)
            squares(3)
            for j in range(4):
                act.wait_ge(turned, 12 + j + 1)
                act.activation(xTf[:, 2 * j:2 * j + 2, :], ps[:, 4 + j, :].rearrange("p (c t) -> p c t", c=2),
                               ACT.Copy).then_inc(xh_done, 1)
            act.activation(xs_hi, xs[:, :, :], ACT.Copy).then_inc(xsh_done, 1)
            act.wait_ge(gd_ready, 1)
            act.activation(ge[:, :], gd[:, :], ACT.Exp).then_inc(ge_done, 1)

            def gather_hi(n, r):
                act.wait_ge(gathered, 2 * n + r - 1)
                act.activation(xg_hi[:, 512 * r:512 * (r + 1)], ps[:, 5, :], ACT.Copy).then_inc(gath_hi, 1)

            def y_round(p):
                act.wait_ge(unit_done, PER_PASS * p + DENSE)
                act.wait_ge(selT_done, p + 1)
                act.wait_ge(comb_added, 2 * p + 1)
                act.activation(y_hi.rearrange("p (b n) -> p b n", b=2), ps[:, 6:8, :], ACT.Copy,
                               scale=gate_slot[:, 0:1]).then_inc(yh_done, 1)

            def expert_pass(p, own_gather, g_off):
                for k in range(AHEAD):
                    split_hi(act, DENSE + k, TURNS * p)
                y_round(p)
                if own_gather:
                    for r in range(2):
                        gather_hi(p + g_off, r)
                for k in range(PER_PASS):
                    if k + AHEAD < PER_PASS:
                        split_hi(act, DENSE + k + AHEAD, TURNS * p)
                    c = k // 4
                    if k < 4 * CHUNKS and k % 4 == 1:
                        act.wait_ge(unit_done, PER_PASS * p + DENSE + k + 1)
                        act.wait_ge(mul_done, CHUNKS * p + (c if c >= 2 else 1))
                        act.activation(moe_s[c % 2], ps[:, 2 * (c % 2), :], ACT.Silu).then_inc(silu_done, 1)
                    if k % 4 == 1 and 1 <= c <= CHUNKS:
                        act.wait_ge(act_turned, CHUNKS * p + c + 1)
                        act.activation(act_hi[:, 512 * (c - 1):512 * c], ps[:, 4, :], ACT.Copy).then_inc(ah_done, 1)
                    if not own_gather and k in (31, 35):
                        gather_hi(p + g_off + 1, (k - 31) // 4)

            for r in range(2):
                gather_hi(1, r)
            act.wait_ge(moe_ready, 1)
            with act.Fori(0, E) as e:
                expert_pass(e, False, 1)
            act.wait_ge(routed, 1)
            passes = act.alloc_register("act_passes")
            act.reg_mov(passes, E)
            with act.Fori(0, E) as e:
                n = act.value_load(counts[0:1, bass.ds(e, 1)])
                with act.If(n > SLOTS):
                    expert_pass(act.snap(passes), True, 2)
                    act.reg_add(passes, passes, 1)
                with act.Else():
                    act.nop()
                act.nop()
            p = act.snap(passes)
            y_round(p)
            act.wait_ge(comb_added, 2 * p + 3)
            squares(4)

        @block.vector
        def _(dve):
            own = [0]

            def link(ins):
                own[0] += 1
                ins.then_inc(dve_own, 1)
                dve.wait_ge(dve_own, own[0])

            def tick(k):
                if k + AHEAD < DENSE:
                    split_lo(dve, k + AHEAD)

            def norm_rows(n):
                dve.wait_ge(rstd_ready, n + 1)
                dve.wait_ge(row_in, 16 * (n + 1 + (n >= 3)))
                for t in range(TT):
                    dve.scalar_tensor_tensor(xs[:, t, :], h[:, t, :], rstd[:, t:t + 1], row[:, :],
                                             ALU.mult, ALU.mult).then_inc(xs_ready if n < 4 else fin_ready, 1)

            def turned_lo(n, b0):
                for j in range(4):
                    dve.wait_ge(xh_done, 4 * n + j + 1)
                    dve.tensor_tensor(xT_lo[:, 512 * j:512 * (j + 1)], ps[:, b0 + j, :],
                                      xT_hi[:, 512 * j:512 * (j + 1)].bitcast(F32), ALU.subtract).then_inc(xl_done, 1)

            def residual(n, banks):
                for t in range(TT):
                    for half in range(2):
                        part = h[:, t, 512 * half:512 * (half + 1)]
                        ins = dve.tensor_tensor(part, part, ps[:, banks + 2 * t + half, :], ALU.add)
                        ins.then_inc(res_added, 1)

            for k in range(AHEAD):
                split_lo(dve, k)
            norm_rows(0)
            dve.wait_ge(cst_in, 64)
            dve.tensor_copy(masks[:, :, :], mask_rows.rearrange("p (l t) -> p l t", l=LEVELS)).then_inc(masks_ready, 1)
            dve.wait_ge(vec_turned, 1)
            link(dve.tensor_copy(vecT[:, :, :], ps[:, 0, 0:KD * NV].rearrange("p (k v) -> p k v", k=KD)))
            low = [vecT[:, 0:4, V_LOW + i] for i in range(3)]
            link(dve.tensor_tensor(lowm[:, :], low[0], low[1], ALU.max))
            link(dve.tensor_tensor(lowm[:, :], lowm[:, :], low[2], ALU.max))
            for i in range(3):
                ins = dve.tensor_tensor(lowe[:, i, :], low[i], lowm[:, :], ALU.subtract)
            ins.then_inc(low_dif, 1)
            turned_lo(0, 4)
            dve.wait_ge(low_exp, 1)
            link(dve.tensor_tensor(lows[:, :], lowe[:, 0, :], lowe[:, 1, :], ALU.add))
            link(dve.tensor_tensor(lows[:, :], lows[:, :], lowe[:, 2, :], ALU.add))
            link(dve.reciprocal(lows[:, :], lows[:, :]))
            link(dve.tensor_tensor(lb[:, :], lowe[:, 0, :], lows[:, :], ALU.mult))
            link(dve.tensor_scalar(olb[:, :], lb[:, :], -1.0, 1.0, ALU.mult, ALU.add))
            link(dve.memset(keep, 1.0))
            link(dve.memset(keep.rearrange("p (c t) -> p c t", t=CHUNK)[:, :, 0:1], 0.0))
            link(dve.memset(upad[:, :, 0:TAPS - 1], 0.0))

            def exponents(level):
                if level >= 3:
                    dve.wait_ge(scored, 2 * (level - 2) + 2)
                to = dec[level % 2]
                if level < CROSS:
                    b = 1 << (level - 1)
                    e4 = to.rearrange("p (n a b) -> p n a b", a=2, b=b)
                    s4 = bsum.rearrange("p (n a b) -> p n a b", a=2, b=b)
                    end = s4[:, :, 0, b - 1:b].to_broadcast([P, 512 // b, b])
                    dve.tensor_tensor(e4[:, :, 0, :], end, s4[:, :, 0, :], ALU.subtract)
                    if b < CHUNK:
                        ins = dve.tensor_tensor(e4[:, :, 1, :], s4[:, :, 1, :], end, ALU.subtract)
                    else:
                        ins = dve.tensor_copy(e4[:, :, 1, :], s4[:, :, 1, :])
                    ins.then_inc(e_ready, 1)
                else:
                    e4 = to.rearrange("p (h c t) -> p h c t", h=HEADS, c=4)
                    s4 = bsum.rearrange("p (h c t) -> p h c t", h=HEADS, c=4)
                    off = cross_off[:, :, :].unsqueeze(3).to_broadcast([P, HEADS, 4, CHUNK])
                    dve.tensor_tensor(e4[:, :, 0:2, :], off[:, :, 0:2, :], s4[:, :, 0:2, :], ALU.subtract)
                    dve.tensor_tensor(e4[:, :, 2:4, :], s4[:, :, 2:4, :], off[:, :, 2:4, :],
                                      ALU.add).then_inc(e_ready, 1)

            def decay(level):
                dve.wait_ge(exp_done, level)
                n, b = (512 // (1 << (level - 1)), 1 << (level - 1)) if level < CROSS else (HEADS, P)
                e4 = dec[level % 2].rearrange("p (n a b) -> p n a b", n=n, a=2)
                k4 = k_t.rearrange("p (n a b) -> p n a b", n=n, a=2)
                q4 = ps[:, 2:4, :].rearrange("p c w -> p (c w)").rearrange("p (n a b) -> p n a b", n=n, a=2)
                dve.tensor_tensor(e4[:, :, 0, :], e4[:, :, 0, :], k4[:, :, 0, :], ALU.mult)
                dve.tensor_tensor(e4[:, :, 1, :], e4[:, :, 1, :], q4[:, :, 1, :], ALU.mult).then_inc(dec_ready, 1)

            def pick(level):
                for t in range(TT):
                    dve.wait_ge(scored, 2 * level + t + 1)
                    dve.copy_predicated(sc[:, 2 * t, :, :], masks[:, level, :].unsqueeze(1).to_broadcast([P, HEADS, P]),
                                        ps[:, 4 + t, :].rearrange("p (h t) -> p h t", h=HEADS)).then_inc(masked, 1)

            def conv_half(half):
                a2 = ax.rearrange("p (c t) -> p c t", c=2)
                dve.wait_ge(in_copied, 5 + half)
                dve.wait_ge(unit_done, 10 + 3 * half)
                own[0] += 1
                dve.tensor_tensor(upad[:, :, TAPS - 1:], ps[:, 1 - half, :].rearrange("p (c t) -> p c t", c=2), a2,
                                  ALU.mult).then_inc(dve_own, 1)
                dve.wait_ge(dve_own, own[0])
                for tap in range(TAPS):
                    for c in range(2):
                        wt = vecT[:, 2 * half + c, V_CW + tap:V_CW + tap + 1]
                        if tap == 0:
                            ins = dve.tensor_scalar(a2[:, c, :], upad[:, c, 0:T], wt, None, ALU.mult)
                        else:
                            ins = dve.scalar_tensor_tensor(a2[:, c, :], upad[:, c, tap:tap + T], wt, a2[:, c, :],
                                                           ALU.mult, ALU.add)
                        if c:
                            link(ins)
                ins = None

            def gate_half(half):
                dve.wait_ge(unit_done, 11 + 3 * half)
                dve.tensor_tensor(ax, ax, ps[:, half, :], ALU.mult).then_inc(ab_read, 1)
                dve.wait_ge(ya_hi, half + 1)
                dve.tensor_tensor(act_lo[:, 512 * half:512 * (half + 1)], ax,
                                  act_hi[:, 512 * half:512 * (half + 1)].bitcast(F32), ALU.subtract).then_inc(ya_lo, 1)

            for k in range(N_IN):
                tick(k)
                if k == 1:
                    dve.wait_ge(sig_done, 2)
                    for hd in range(HEADS):
                        part = dec[0][:, T * hd:T * (hd + 1)]
                        ins = dve.tensor_scalar(part, part, olb[:, hd:hd + 1], lb[:, hd:hd + 1], ALU.mult, ALU.add)
                    ins.then_inc(fg_ready, 1)
                    dve.wait_ge(fg_ready, 1)
                    dve.tensor_scalar(k_t, dec[0], -1.0, 1.0, ALU.mult, ALU.add).then_inc(k_ready, 1)
                if k == 2:
                    dve.wait_ge(ln_done, 1)
                    link(dve.tensor_tensor_scan(bsum, keep, dec[1], 0.0, ALU.mult, ALU.add))
                    exponents(1)
                    last = bsum.rearrange("p (h c t) -> p h c t", h=HEADS, c=4)[:, :, :, CHUNK - 1]
                    off = cross_off[:, :, :]
                    dve.tensor_tensor(off[:, :, 0:1], last[:, :, 0:1], last[:, :, 1:2], ALU.add)
                    dve.tensor_copy(off[:, :, 1:2], last[:, :, 1:2])
                    dve.memset(off[:, :, 2:3], 0.0)
                    dve.tensor_copy(off[:, :, 3:4], last[:, :, 2:3])
                    link(dve.memset(sc[:, :, :, :], 0.0))
                if 4 <= k <= 11:
                    decay(k - 3)
                    pick(k - 4)
                    if k - 2 <= CROSS:
                        exponents(k - 2)
                if k == 9 or k == 12:
                    conv_half((k - 9) // 3)
                if k == 10 or k == 13:
                    gate_half((k - 10) // 3)
                if k == 12:
                    dve.wait_ge(cst_in, 64)
                    dve.wait_ge(g_silu, 1)
                    link(dve.tensor_tensor(row[:, :].rearrange("p (g c) -> p g c", c=P),
                                           row[:, :].rearrange("p (g c) -> p g c", c=P),
                                           gnorm_row[:, :].unsqueeze(1).to_broadcast([P, 8, P]), ALU.mult))
            for j in range(N_OUT):
                tick(U_OUT + j)
                if j == 0:
                    for t in range(TT):
                        dve.wait_ge(o_sq, t + 1)
                        dve.reduce_sum(oss[:, HEADS * t:HEADS * (t + 1)],
                                       osq[:, 512 * t:512 * (t + 1)].rearrange("p (h c) -> p h c", h=HEADS),
                                       AX.X).then_inc(o_sum, 1)
                    dve.wait_ge(o_rstd, 1)
                    for t in range(TT):
                        for hd in range(HEADS):
                            part = slice(P * hd, P * (hd + 1))
                            ins = dve.scalar_tensor_tensor(yb[:, t, part], ps[:, 6 + t, part],
                                                           orstd[:, HEADS * t + hd:HEADS * t + hd + 1],
                                                           gq[:, t, part], ALU.mult, ALU.mult)
                        ins.then_inc(yb_ready, 1)
                if j == 1:
                    for b in range(2):
                        dve.wait_ge(yb_hi, b + 1)
                        dve.tensor_tensor(act_lo[:, D + 512 * b:D + 512 * (b + 1)], ps[:, 4 + b, :],
                                          act_hi[:, D + 512 * b:D + 512 * (b + 1)].bitcast(F32),
                                          ALU.subtract).then_inc(yb_lo, 1)
            dve.wait_ge(unit_done, U_UP)
            residual(0, 0)
            norm_rows(1)
            turned_lo(1, 4)

            def up_ticks(m, i=0):
                k = U_UP + 2 * m
                split_lo(dve, k + AHEAD, i)
                split_lo(dve, k + 1 + AHEAD, i)
                dve.wait_ge(unit_done, RAW * i + k + 2)
                dve.wait_ge(up_silu, 3 * i + m + 1)
                dve.tensor_tensor(up_p[m % 3], up_s[m % 3], ps[:, 2 * (m % 3) + 1, :], ALU.mult).then_inc(up_mul, 1)
                dve.wait_ge(up_hi, 3 * i + m + 1)
                dve.tensor_tensor(act_lo[:, bass.ds(i * 1536 + 512 * m, 512)], up_p[m % 3],
                                  act_hi[:, bass.ds(i * 1536 + 512 * m, 512)].bitcast(F32),
                                  ALU.subtract).then_inc(up_lo, 1)

            with dve.Fori(0, PAIRS // 3) as i:
                for m in range(3):
                    up_ticks(m, i)
            for m in range(PAIRS // 3 * 3, PAIRS):
                up_ticks(m)
            for j in range(N_DOWN):
                tick(U_DOWN + j)
            dve.wait_ge(unit_done, U_PW1)
            residual(1, 4)
            norm_rows(2)
            dve.memset(glu[:, :, 0:PAD], 0.0)
            turned_lo(2, 0)
            todo = []
            steps = [0]

            def conv_taps(n):
                for c, tap in todo[:n]:
                    wt = vecT[:, c, V_DW + tap:V_DW + tap + 1]
                    if steps[0] >= 2:
                        dve.wait_ge(conv_step, steps[0] - 1)
                    if tap == 0:
                        ins = dve.tensor_scalar(dwc[:, c, :], glu[:, c, 0:T], wt, vecT[:, c, V_BDW:V_BDW + 1],
                                                ALU.mult, ALU.add)
                    else:
                        ins = dve.scalar_tensor_tensor(dwc[:, c, :], glu[:, c, tap:tap + T], wt, dwc[:, c, :],
                                                       ALU.mult, ALU.add)
                    ins.then_inc(conv_step, 1)
                    steps[0] += 1
                del todo[:n]

            for j in range(N_PW1 // 2):
                tick(U_PW1 + 2 * j)
                conv_taps(9)
                tick(U_PW1 + 2 * j + 1)
                dve.wait_ge(sg_done, 2 * (j + 1))
                for m in range(2):
                    c = 2 * j + m
                    dve.scalar_tensor_tensor(glu[:, c, PAD:], ps[:, 4 + 2 * (j % 2), T * m:T * (m + 1)],
                                             vecT[:, c, V_BA:V_BA + 1], sg[j % 2][:, T * m:T * (m + 1)],
                                             ALU.add, ALU.mult).then_inc(glu_done, 1)
                dve.wait_ge(glu_done, 2 * (j + 1))
                todo.extend((2 * j + m, tap) for tap in range(CONF_K) for m in range(2))
                conv_taps(9)
            dve.wait_ge(row_in, 64)
            for t in range(TT):
                dve.tensor_tensor(h[:, t, :], h[:, t, :], row[:, :], ALU.add).then_inc(bias_added, 1)
            conv_taps(len(todo))
            for t in range(TT):
                dve.wait_ge(conv_turned, t + 1)
                for half in range(2):
                    ins = dve.bn_stats(lnst[:, t, half, :], ps[:, 2 * t + half, :])
                link(ins)
                ins = dve.bn_aggr(lnmv[:, t, :], lnst[:, t, :, :].rearrange("p a b -> p (a b)"))
            ins.then_inc(ln_var, 1)
            dve.wait_ge(ln_rstd, 1)
            for t in range(TT):
                dve.tensor_scalar(xs[:, t, :].rearrange("p (b n) -> p b n", b=2), ps[:, 2 * t:2 * t + 2, :],
                                  lnmv[:, t, 0:1], rstd[:, t:t + 1],
                                  ALU.subtract, ALU.mult).then_inc(ln_ready, 1)
            for j in range(4):
                dve.wait_ge(z_hi, j + 1)
                dve.tensor_tensor(act_lo[:, 512 * j:512 * (j + 1)], zz[j % 2],
                                  act_hi[:, 512 * j:512 * (j + 1)].bitcast(F32), ALU.subtract).then_inc(z_lo, 1)
            for j in range(N_PW2):
                tick(U_PW2 + j)
            dve.wait_ge(unit_done, DENSE)
            dve.wait_ge(bias_added, 2)
            residual(2, 0)
            norm_rows(3)
            dve.wait_ge(xsh_done, 1)
            dve.tensor_tensor(xs_lo, xs[:, :, :], xs_hi.bitcast(F32), ALU.subtract).then_inc(xsl_done, 1)
            dve.wait_ge(logits_done, 1)
            link(dve.tensor_copy(lg[:, :, :], ps[:, 0, 0:TT * E].rearrange("p (t e) -> p t e", t=TT)))
            for t in range(TT):
                ins = dve.max(top[:, t, :], lg[:, t, :])
            link(ins)
            for t in range(TT):
                ins = dve.max_index(topi[:, t, :], top[:, t, :], lg[:, t, :])
            dve.tensor_tensor(gd[:, :].unsqueeze(2), top[:, :, 1:2], top[:, :, 0:1], ALU.subtract).then_inc(gd_ready, 1)
            link(ins)
            link(dve.tensor_copy(topf[:, :, :], topi[:, :, 0:2]))
            for i in range(2):
                for t in range(TT):
                    ins = dve.tensor_scalar(oh[:, i, t, :], iota[:, 0:E], topf[:, t, i:i + 1], None, ALU.is_equal)
            link(ins)
            dve.tensor_tensor(msk[:, :, :], oh[:, 0, :, :], oh[:, 1, :, :], ALU.add).then_inc(mask_ready, 1)
            dve.wait_ge(ge_done, 1)
            link(dve.tensor_scalar(gd[:, :], ge[:, :], 1.0, None, ALU.add))
            link(dve.reciprocal(g12[:, :, 0], gd[:, :]))
            link(dve.tensor_tensor(g12[:, :, 1], ge[:, :], g12[:, :, 0], ALU.mult))
            for t in range(TT):
                ins = dve.tensor_scalar(gate[:, t, 0:E], oh[:, 0, t, :], g12[:, t, 0:1], None, ALU.mult)
            link(ins)
            for t in range(TT):
                ins = dve.scalar_tensor_tensor(gate[:, t, 0:E], oh[:, 1, t, :], g12[:, t, 1:2], gate[:, t, 0:E],
                                               ALU.mult, ALU.add)
            link(ins)
            dve.tensor_copy(gate[:, :, E + 1:RC], gate[:, :, 0:E])
            dve.memset(gate[:, :, E:E + 1], 0.0).then_inc(mul_done, 1)
            dve.memset(rank[:, :, E:E + 1], -1.0).then_inc(al_done, 1)
            dve.wait_ge(rank_done, 1)
            dve.wait_ge(mask_ready, 1)
            ranks = ps[:, 1, 0:TT * E].rearrange("p (t e) -> p t e", t=TT)
            for t in range(TT):
                ins = dve.scalar_tensor_tensor(rank[:, t, 0:E], ranks[:, t, :], 1.0, msk[:, t, :], ALU.add, ALU.mult)
            link(ins)
            link(dve.tensor_scalar(rank[:, :, 0:E], rank[:, :, 0:E], -1.0, None, ALU.add))
            link(dve.tensor_scalar(rank[:, :, E + 1:RC], rank[:, :, 0:E], float(-SLOTS), None, ALU.add))
            dve.tensor_copy(counts[:, :], ps[:, 1, TT * E:(TT + 1) * E]).then_inc(routed, 1)

            def select(col):
                for t in range(TT):
                    at = rank[:, t, bass.ds(col, 1)]
                    dve.tensor_scalar(selg[:, t, :], iota, at, gate[:, t, bass.ds(col, 1)], ALU.is_equal, ALU.mult)
                    ins = dve.tensor_scalar(sel[:, t, :], iota, at, None, ALU.is_equal)
                ins.then_inc(sel_ready, 1)

            def gather_lo(n, r):
                dve.wait_ge(gath_hi, 2 * n + r - 1)
                dve.tensor_tensor(xg_lo[:, 512 * r:512 * (r + 1)], ps[:, 5, :],
                                  xg_hi[:, 512 * r:512 * (r + 1)].bitcast(F32), ALU.subtract).then_inc(gath_lo, 1)

            def y_rest(p):
                dve.wait_ge(yh_done, p + 1)
                dve.scalar_tensor_tensor(y_lo.rearrange("p (b n) -> p b n", b=2), ps[:, 6:8, :], gate_slot[:, 0:1],
                                         y_hi.rearrange("p (b n) -> p b n", b=2).bitcast(F32),
                                         ALU.mult, ALU.subtract).then_inc(yl_done, 1)

            def add_combined(p, t):
                dve.wait_ge(comb_done, 2 * p + t + 1)
                for half in range(2):
                    part = h[:, t, 512 * half:512 * (half + 1)]
                    ins = dve.tensor_tensor(part, part, ps[:, 5 - half, :], ALU.add)
                ins.then_inc(comb_added, 1)

            def expert_pass(p, e, own_gather, g_off):
                for k in range(AHEAD):
                    split_lo(dve, DENSE + k, TURNS * p)
                y_rest(p)
                if own_gather:
                    select(e)
                    for r in range(2):
                        gather_lo(p + g_off, r)
                for k in range(PER_PASS):
                    if k + AHEAD < PER_PASS:
                        split_lo(dve, DENSE + k + AHEAD, TURNS * p)
                    c = k // 4
                    if k % 4 == 1 and 1 <= c <= CHUNKS:
                        dve.wait_ge(ah_done, CHUNKS * p + c)
                        dve.tensor_tensor(act_lo[:, 512 * (c - 1):512 * c], ps[:, 4, :],
                                          act_hi[:, 512 * (c - 1):512 * c].bitcast(F32), ALU.subtract).then_inc(al_done, 1)
                    if k < 4 * CHUNKS and k % 4 == 3:
                        dve.wait_ge(unit_done, PER_PASS * p + DENSE + k + 1)
                        dve.wait_ge(silu_done, CHUNKS * p + c + 1)
                        dve.wait_ge(act_turned, CHUNKS * p + (c if c >= 2 else 1))
                        dve.tensor_tensor(moe_p[c % 2], moe_s[c % 2], ps[:, 2 * (c % 2) + 1, :],
                                          ALU.mult).then_inc(mul_done, 1)
                    if k == 4:
                        add_combined(p, 0)
                    if k == 8:
                        add_combined(p, 1)
                    if k == 16:
                        dve.wait_ge(selg_turned, p + 1)
                        dve.reduce_sum(gate_slot[:, :], ps[:, 5, 0:T], AX.X)
                        dve.tensor_scalar(selT[:, :], ps[:, 5, 0:T], 0.0, None, ALU.is_gt).then_inc(selT_done, 1)
                    if not own_gather and k == 20:
                        select(e + 1)
                    if not own_gather and k in (31, 35):
                        gather_lo(p + g_off + 1, (k - 31) // 4)

            dve.memset(ps[:, 6:8, :], 0.0).then_inc(moe_ready, 1)
            dve.memset(gate_slot[:, :], 0.0).then_inc(comb_added, 1)
            dve.memset(selT[:, :].bitcast(F32), 0.0).then_inc(selT_done, 1)
            select(0)
            for r in range(2):
                gather_lo(1, r)
            with dve.Fori(0, E) as e:
                expert_pass(e, e, False, 1)
            passes = dve.alloc_register("dve_passes")
            dve.reg_mov(passes, E)
            dve.wait_ge(routed, 1)
            with dve.Fori(0, E) as e:
                n = dve.value_load(counts[0:1, bass.ds(e, 1)])
                with dve.If(n > SLOTS):
                    expert_pass(dve.snap(passes), e + (E + 1), True, 2)
                    dve.reg_add(passes, passes, 1)
                with dve.Else():
                    dve.nop()
                dve.nop()
            p = dve.snap(passes)
            y_rest(p)
            for t in range(TT):
                add_combined(p, t)
            norm_rows(4)

        @block.tensor
        def _(pe):
            def three(into, a_hi, a_lo, b_hi, b_lo, start, stop):
                pe.matmul(into, a_hi, b_hi, start=start, stop=False)
                pe.matmul(into, a_hi, b_lo, start=False, stop=False)
                return pe.matmul(into, a_lo, b_hi, start=False, stop=stop)

            def by_channel(k, bank, turn=0):
                pe.wait_ge(lo_done, RAW * turn + k + 1)
                for m in range(2):
                    for c in range(KD):
                        at = slice(256 * c + P * m, 256 * c + P * (m + 1))
                        ins = three(ps[:, bank, T * m:T * (m + 1)], hi_unit(k)[:, at], lo_unit(k)[:, at],
                                    xT_hi[:, T * c:T * (c + 1)], xT_lo[:, T * c:T * (c + 1)], c == 0, c == KD - 1)
                ins.then_inc(unit_done, 1)

            def by_token(k, bank):
                pe.wait_ge(lo_done, k + 1)
                for t in range(TT):
                    for c in range(KD):
                        at = slice(T * c + P * t, T * c + P * (t + 1))
                        wt = slice(256 * c, 256 * (c + 1))
                        ins = three(ps[:, bank, 256 * t:256 * (t + 1)], xT_hi[:, at], xT_lo[:, at],
                                    hi_unit(k)[:, wt], lo_unit(k)[:, wt], c == 0, c == KD - 1)
                ins.then_inc(unit_done, 1)

            def to_stream(k, j, n, banks):
                pe.wait_ge(lo_done, k + 1)
                for r in range(2):
                    for t in range(TT):
                        at = slice(T * (2 * j + r) + P * t, T * (2 * j + r) + P * (t + 1))
                        for half in range(2):
                            wt = slice(D * r + 512 * half, D * r + 512 * (half + 1))
                            ins = three(ps[:, banks + 2 * t + half, :], act_hi[:, at], act_lo[:, at],
                                        hi_unit(k)[:, wt], lo_unit(k)[:, wt], j == 0 and r == 0, j == n - 1 and r == 1)
                ins.then_inc(unit_done, 1)

            def turn_stream(n, b0):
                for t in range(TT):
                    pe.wait_ge(xs_ready, 2 * n + t + 1)
                    for c in range(KD):
                        ins = pe.transpose(ps[:, b0 + c // 2, T * (c % 2) + P * t:T * (c % 2) + P * (t + 1)],
                                           xs[:, t, P * c:P * (c + 1)], ident)
                        if t == TT - 1 and c % 2:
                            ins.then_inc(turned, 1)

            def score(level):
                if level == 0:
                    pe.wait_ge(q_copied, 1)
                    pe.wait_ge(k_ready, 1)
                else:
                    pe.wait_ge(dec_ready, level)
                a = k_t if level == 0 else dec[level % 2]
                b = dec[level % 2]
                for t in range(TT):
                    if level:
                        pe.wait_ge(masked, 2 * (level - 1) + t + 1)
                    for hd in range(HEADS):
                        at = slice(T * hd + P * t, T * hd + P * (t + 1))
                        ins = pe.matmul(ps[:, 4 + t, P * hd:P * (hd + 1)], a[:, at], b[:, at], start=True, stop=True)
                    ins.then_inc(scored, 1)

            pe.wait_ge(cst_in, 64)
            pe.wait_ge(vec_in, 16 * 9)
            for c in range(KD):
                ins = pe.transpose(ps[:, 0, NV * c:NV * (c + 1)], vec_rows[:, P * c:P * (c + 1)], ident[0:NV, 0:NV])
            ins.then_inc(vec_turned, 1)
            turn_stream(0, 4)
            banks = [0, 1, 2, 3, 0, 1, 0, 1, 0, 1, 0, 1, 0, 1]
            pe.wait_ge(xl_done, 4)
            pe.wait_ge(dve_own, 1)
            for k in range(N_IN):
                if k in (4, 5):
                    pe.wait_ge(sig_done, k - 3)
                if k in (6, 7, 8, 9):
                    pe.wait_ge(in_copied, k - 5)
                if k == 10:
                    pe.wait_ge(in_copied, 5)
                if k == 11:
                    pe.wait_ge(ab_read, 1)
                if k == 12:
                    pe.wait_ge(ab_read, 1)
                if k == 13:
                    pe.wait_ge(in_copied, 6)
                if k in (4, 5, 6, 7):
                    by_token(k, banks[k])
                else:
                    by_channel(k, banks[k])
                if 4 <= k <= 11:
                    score(k - 4)
                if k == 12:
                    pe.wait_ge(dec_ready, CROSS)
                    pe.wait_ge(masked, 2 * LEVELS)
                    for hd in range(HEADS):
                        ins = pe.matmul(ps[:, 4, P * hd:P * (hd + 1)], dec[0][:, T * hd:T * hd + P],
                                        dec[0][:, T * hd + P:T * (hd + 1)], start=True, stop=True)
                    ins.then_inc(scored, 1)
            pe.wait_ge(cross_copied, 1)
            for hd in range(HEADS):
                at = slice(P * hd, P * (hd + 1))
                ins = pe.matmul(ps[:, 6, at], sc[:, 0, hd, :], v_t[:, 0, at], start=True, stop=True)
            ins.then_inc(o_done, 1)
            for hd in range(HEADS):
                at = slice(P * hd, P * (hd + 1))
                pe.matmul(ps[:, 7, at], sc[:, 1, hd, :], v_t[:, 0, at], start=True, stop=False)
                ins = pe.matmul(ps[:, 7, at], sc[:, 2, hd, :], v_t[:, 1, at], start=False, stop=True)
            ins.then_inc(o_done, 1)
            pe.wait_ge(ya_lo, 2)
            to_stream(U_OUT, 0, N_OUT, 0)
            to_stream(U_OUT + 1, 1, N_OUT, 0)
            for t in range(TT):
                pe.wait_ge(yb_ready, t + 1)
                for hd in range(HEADS):
                    ins = pe.transpose(ps[:, 4 + hd // 2, T * (hd % 2) + P * t:T * (hd % 2) + P * (t + 1)],
                                       yb[:, t, P * hd:P * (hd + 1)], ident)
                    if t == TT - 1 and hd % 2:
                        ins.then_inc(yb_turned, 1)
            for b in range(2):
                pe.wait_ge(yb_lo, b + 1)
                to_stream(U_OUT + 2 + b, 2 + b, N_OUT, 0)
            turn_stream(1, 4)
            pe.wait_ge(xl_done, 8)

            def up_pair(m, i=0, first=False):
                if not first:
                    pe.wait_ge(up_mul, 3 * i + m - 2)
                by_channel(U_UP + 2 * m, 2 * (m % 3), i)
                by_channel(U_UP + 2 * m + 1, 2 * (m % 3) + 1, i)

            for m in range(3):
                up_pair(m, 0, True)
            with pe.Fori(1, PAIRS // 3) as i:
                for m in range(3):
                    up_pair(m, i)
            for m in range(PAIRS // 3 * 3, PAIRS):
                up_pair(m)
            pe.wait_ge(up_mul, PAIRS - 2)
            for j in range(N_DOWN):
                pe.wait_ge(up_lo, j + 1)
                to_stream(U_DOWN + j, j, N_DOWN, 4)
            turn_stream(2, 0)
            pe.wait_ge(xl_done, 12)
            for j in range(N_PW1 // 2):
                if j >= 2:
                    pe.wait_ge(glu_done, 2 * (j - 1))
                by_channel(U_PW1 + 2 * j, 4 + 2 * (j % 2))
                by_channel(U_PW1 + 2 * j + 1, 5 + 2 * (j % 2))
            pe.wait_ge(conv_step, CONF_K * KD)
            for t in range(TT):
                for c in range(KD):
                    ins = pe.transpose(ps[:, 2 * t + c // 4, P * (c % 4):P * (c % 4 + 1)],
                                       dwc[:, c, P * t:P * (t + 1)], ident)
                ins.then_inc(conv_turned, 1)
            for t in range(TT):
                pe.wait_ge(ln_ready, t + 1)
                for c in range(KD):
                    ins = pe.transpose(ps[:, 4 + c // 2, T * (c % 2) + P * t:T * (c % 2) + P * (t + 1)],
                                       xs[:, t, P * c:P * (c + 1)], ident)
                    if t == TT - 1 and c % 2:
                        ins.then_inc(ln_turned, 1)
            for j in range(N_PW2):
                pe.wait_ge(z_lo, j + 1)
                to_stream(U_PW2 + j, j, N_PW2, 0)
            turn_stream(3, 4)
            pe.wait_ge(xh_done, 16)
            pe.wait_ge(res_added, 12)
            for t in range(TT):
                for c in range(KD):
                    ins = pe.matmul(ps[:, 0, E * t:E * (t + 1)], xTf[:, c, P * t:P * (t + 1)], router[:, c, :],
                                    start=c == 0, stop=c == KD - 1)
            ins.then_inc(logits_done, 1)
            pe.wait_ge(mask_ready, 1)
            pe.matmul(ps[:, 1, 0:E], upper, msk[:, 0, :], start=True, stop=True).then_inc(act_turned, 1)
            pe.matmul(ps[:, 1, E:2 * E], ones, msk[:, 0, :], start=True, stop=False)
            pe.matmul(ps[:, 1, E:2 * E], upper, msk[:, 1, :], start=False, stop=True)
            pe.matmul(ps[:, 1, 2 * E:3 * E], ones, msk[:, 0, :], start=True, stop=False)
            pe.matmul(ps[:, 1, 2 * E:3 * E], ones, msk[:, 1, :], start=False, stop=True).then_inc(rank_done, 1)

            def gather(n, r, ready):
                pe.wait_ge(sel_ready, ready)
                if r:
                    pe.wait_ge(gath_lo, 2 * n - 1)
                for c in range(4):
                    ch = slice(512 * r + P * c, 512 * r + P * (c + 1))
                    for t in range(TT):
                        pe.matmul(ps[:, 5, P * c:P * (c + 1)], xs_hi[:, t, ch], sel[:, t, :], start=t == 0, stop=False)
                        ins = pe.matmul(ps[:, 5, P * c:P * (c + 1)], xs_lo[:, t, ch], sel[:, t, :],
                                        start=False, stop=t == TT - 1)
                ins.then_inc(gathered, 1)

            def combine(p, t):
                if t == 0:
                    pe.wait_ge(yl_done, p + 1)
                    pe.wait_ge(comb_added, 2 * p + 1)
                    pe.wait_ge(al_done, CHUNKS * p + 1)
                else:
                    pe.wait_ge(comb_added, 2 * p + 2)
                for half in range(2):
                    at = slice(512 * half, 512 * (half + 1))
                    pe.matmul(ps[:, 5 - half, :], selT[:, P * t:P * (t + 1)], y_hi[:, at], start=True, stop=False)
                    ins = pe.matmul(ps[:, 5 - half, :], selT[:, P * t:P * (t + 1)], y_lo[:, at], start=False, stop=True)
                ins.then_inc(comb_done, 1)

            def expert_pass(p, own_gather, g_off):
                if own_gather:
                    pe.wait_ge(selT_done, p + 1)
                    for r in range(2):
                        gather(p + g_off, r, p + g_off)
                pe.wait_ge(gath_lo, 2 * (p + g_off))
                for k in range(PER_PASS):
                    c = k // 4
                    if k < 4 * CHUNKS:
                        if k % 4 == 0:
                            pe.wait_ge(mul_done, CHUNKS * p + (c if c >= 2 else 1))
                        pe.wait_ge(lo_done, PER_PASS * p + DENSE + k + 1)
                        for r in range(4):
                            ch = 4 * (k % 2) + r
                            at = slice(SLOTS * ch, SLOTS * (ch + 1))
                            wt = slice(512 * r, 512 * (r + 1))
                            ins = three(ps[:, 2 * (c % 2) + (k % 4) // 2, :], xg_hi[:, at], xg_lo[:, at],
                                        hi_unit(DENSE + k)[:, wt], lo_unit(DENSE + k)[:, wt], ch == 0, ch == KD - 1)
                        ins.then_inc(unit_done, 1)
                    else:
                        j = k - 4 * CHUNKS
                        if j == 0:
                            pe.wait_ge(yl_done, p + 1)
                        pe.wait_ge(al_done, CHUNKS * p + j // 2 + 2)
                        pe.wait_ge(lo_done, PER_PASS * p + DENSE + k + 1)
                        for r in range(2):
                            at = slice(SLOTS * (2 * j + r), SLOTS * (2 * j + r + 1))
                            for half in range(2):
                                wt = slice(D * r + 512 * half, D * r + 512 * (half + 1))
                                ins = three(ps[:, 6 + half, :], act_hi[:, at], act_lo[:, at],
                                            hi_unit(DENSE + k)[:, wt], lo_unit(DENSE + k)[:, wt],
                                            j == 0 and r == 0, k == PER_PASS - 1 and r == 1)
                        ins.then_inc(unit_done, 1)
                    if k == 3:
                        combine(p, 0)
                    if k == 7:
                        pe.wait_ge(al_done, CHUNKS * p + 2)
                        combine(p, 1)
                    if k % 4 == 1 and 1 <= c <= CHUNKS:
                        pe.wait_ge(mul_done, CHUNKS * p + c + 1)
                        if c == 1:
                            pe.wait_ge(comb_added, 2 * p + 2)
                        elif c == 2:
                            pe.wait_ge(comb_added, 2 * p + 3)
                        else:
                            pe.wait_ge(al_done, CHUNKS * p + c)
                        for i in range(4):
                            ins = pe.transpose(ps[:, 4, P * i:P * (i + 1)], moe_p[(c - 1) % 2][:, P * i:P * (i + 1)], ident)
                        ins.then_inc(act_turned, 1)
                    if k == 15:
                        pe.wait_ge(sel_ready, p + g_off)
                        for t in range(TT):
                            ins = pe.transpose(ps[:, 5, P * t:P * (t + 1)], selg[:, t, :], ident)
                        ins.then_inc(selg_turned, 1)
                    if not own_gather and k == 31:
                        pe.wait_ge(selT_done, p + 2)
                        gather(p + g_off + 1, 0, p + g_off + 1)
                    if not own_gather and k == 35:
                        gather(p + g_off + 1, 1, p + g_off + 1)

            pe.wait_ge(xsl_done, 1)
            for r in range(2):
                gather(1, r, 1)
            with pe.Fori(0, E) as e:
                expert_pass(e, False, 1)
            passes = pe.alloc_register("pe_passes")
            pe.reg_mov(passes, E)
            pe.wait_ge(routed, 1)
            with pe.Fori(0, E) as e:
                n = pe.value_load(counts[0:1, bass.ds(e, 1)])
                with pe.If(n > SLOTS):
                    expert_pass(pe.snap(passes), True, 2)
                    pe.reg_add(passes, passes, 1)
                with pe.Else():
                    pe.nop()
                pe.nop()
            p = pe.snap(passes)
            combine(p, 0)
            combine(p, 1)


_INS = ['x', 'ev_norm_mix', 'ev_w_in', 'ev_conv_w', 'hgrn_lower_bounds', 'ev_gnorm', 'ev_w_out',
        'ev_norm_ffn', 'ev_ffn_w1', 'ev_ffn_w3', 'ev_ffn_w2', 'od_norm_mix', 'od_w_pw1', 'od_b_pw1',
        'od_w_dw', 'od_b_dw', 'od_ln_g', 'od_ln_b', 'od_w_pw2', 'od_b_pw2', 'od_norm_ffn',
        'od_router', 'od_moe_w1', 'od_moe_w3', 'od_moe_w2', 'final_norm']


def kernel(**inputs):
    import concourse.bacc as bacc
    from concourse.bass_utils import run_bass_kernel_spmd

    nc = bacc.Bacc("TRN2", target_bir_lowering=False, num_devices=1, dynamic_dma_scratch_size=2048)
    arrays = {f"in_{name}": np.ascontiguousarray(inputs[name]) for name in _INS}
    arrays["in_const_f32"], arrays["in_const_masks"] = constants()
    args = [nc.dram_tensor(name, a.shape, mybir.dt.from_np(a.dtype), kind="ExternalInput").ap()
            for name, a in arrays.items()]
    args.append(nc.dram_tensor("out_0", (1, T, D), F32, kind="ExternalOutput").ap())
    build_program(nc, *args)
    r = run_bass_kernel_spmd(nc, [arrays], core_ids=[0])
    return r.results[0]["out_0"]
```

```python
from contextlib import ExitStack

import numpy as np

import concourse.bass as bass
from concourse import mybir

P = 128
F32 = mybir.dt.float32
F32R = mybir.dt.float32r
U8 = mybir.dt.uint8
U32 = mybir.dt.uint32
I32 = mybir.dt.int32
ALU = mybir.AluOpType
ACT = mybir.ActivationFunctionType
AX = mybir.AxisListType

EPS = 1e-6
T = 256
TT = T // P
D = 1024
KD = D // P
CONV = 512
HEADS = 4
TAPS = 3
CHUNK = 64
CONF_K = 31
FF = 2816
FE = 3584
E = 8
SLOTS = P
PAD = CONF_K - 1
OWN_TAPS = [CONF_K] * 4 + [29, 8, 20, 1]
SHARED = [c for c in range(KD) if OWN_TAPS[c] < CONF_K]
PE_TAPS = [(c, tap) for c in SHARED for tap in range(OWN_TAPS[c], CONF_K)]
DIAGS = 8


def tap_order(odd, start):
    tiles = range(odd, KD, 2)
    steps = [(start[i] + tap, c, tap) for i, c in enumerate(tiles) for tap in range(OWN_TAPS[c])]
    return [(c, tap) for _, c, tap in sorted(steps)]


DVE_ORDER = tap_order(0, [0, 18, 33, 44])
MADE_ORDER = tap_order(1, [0, 15, 29, 30])
POOL_ORDER = [(c, tap) for c, tap in MADE_ORDER if tap]
PRODUCTS = 8

UNIT = 2048
RAW = 6
SPLIT = 3
AHEAD = 2
N_IN, N_OUT, N_UP, N_DOWN, N_PW1, N_PW2 = 14, 4, 22, 11, 8, 4
U_OUT = N_IN
U_UP = U_OUT + N_OUT
U_DOWN = U_UP + N_UP
U_PW1 = U_DOWN + N_DOWN
U_PW2 = U_PW1 + N_PW1
DENSE = U_PW2 + N_PW2
CHUNKS = FE // 512
PER_PASS = 4 * CHUNKS + FE // 256
PAIRS = FF // 256
assert PER_PASS % RAW == 0 and U_UP % RAW == 0 and RAW % SPLIT == 0 and PER_PASS % SPLIT == 0
TURNS = PER_PASS // RAW

AX0, AB0, AC0, Q0, F0, I0, G0 = (512 * i for i in range(7))
IN_COLS = [F0, F0 + 256, Q0, Q0 + 256, I0, I0 + 256, G0, G0 + 256,
           AX0, AC0, AB0, AX0 + 256, AC0 + 256, AB0 + 256]

V_BDW, V_LNG, V_LNB, V_BA, V_BB, V_LOW, V_CW, V_DW = 0, 1, 2, 3, 4, 5, 8, 11
NV = V_DW + CONF_K

LEVELS = 8
CROSS = LEVELS
RC = 2 * E + 1


def constants():
    s, t = np.arange(P)[:, None], np.arange(P)[None, :]
    flat = [np.eye(P), s < t, np.ones((P, P)), np.broadcast_to(t, (P, P))]
    masks = [s == t]
    for b in (1 << np.arange(LEVELS - 1)):
        masks.append((s // (2 * b) == t // (2 * b)) & (s // b % 2 == 0) & (t // b % 2 == 1))
    return (np.concatenate([np.asarray(m, np.float32) for m in flat], 1),
            np.concatenate([np.asarray(m, np.float32) for m in masks], 1))


def build_program(nc, x, ev_norm_mix, ev_w_in, ev_conv_w, hgrn_lower_bounds, ev_gnorm, ev_w_out,
                  ev_norm_ffn, ev_ffn_w1, ev_ffn_w3, ev_ffn_w2, od_norm_mix, od_w_pw1, od_b_pw1,
                  od_w_dw, od_b_dw, od_ln_g, od_ln_b, od_w_pw2, od_b_pw2, od_norm_ffn, od_router,
                  od_moe_w1, od_moe_w3, od_moe_w2, final_norm, const_f32, const_masks, out):
    with ExitStack() as ctx:
        def sb(name, shape, dt=F32):
            return ctx.enter_context(nc.sbuf_tensor(name, shape, dt))

        def sem(name):
            return ctx.enter_context(nc.semaphore(name))

        raw = sb("raw", [P, RAW, UNIT])
        w_hi = sb("w_hi", [P, SPLIT, UNIT], F32R)
        w_lo = sb("w_lo", [P, SPLIT, UNIT], F32R)
        xT_hi = sb("xT_hi", [P, 2 * D], F32R)
        xT_lo = sb("xT_lo", [P, 2 * D], F32R)
        act_hi = sb("act_hi", [P, FF * 2], F32R)
        act_lo = sb("act_lo", [P, FF * 2], F32R)
        sel = sb("sel", [P, TT, SLOTS])
        selT = sb("selT", [SLOTS, T], F32R)
        h = sb("h", [P, TT, D])
        xs = sb("xs", [P, TT, D])
        work = sb("work", [P, 6144])
        row = sb("row", [P, D])
        cst = sb("cst", [P, 4 * P])
        masks = sb("masks", [P, LEVELS, P], U8)
        vecT = sb("vecT", [P, KD, NV])
        router = sb("router", [P, KD, E])
        ss = sb("ss", [P, TT])
        ms = sb("ms", [P, TT])
        rstd = sb("rstd", [P, TT])
        mhalf = sb("mhalf", [P, 8])
        lowm = sb("lowm", [P, 4])
        lowe = sb("lowe", [P, 3, 4])
        lows = sb("lows", [P, 4])
        lb = sb("lb", [P, 4])
        olb = sb("olb", [P, 4])
        cross_off = sb("cross_off", [P, HEADS, 4])
        oss = sb("oss", [P, TT * HEADS])
        orstd = sb("orstd", [P, TT * HEADS])
        lnst = sb("lnst", [P, TT, 2, 6])
        lnmv = sb("lnmv", [P, TT, 2])
        lg = sb("lg", [P, TT, E])
        lgT = sb("lgT", [E, T])
        top = sb("top", [P, TT, 8])
        topi = sb("topi", [P, TT, 8], U32)
        topf = sb("topf", [P, TT, 2])
        gd = sb("gd", [P, TT])
        ge = sb("ge", [P, TT])
        g12 = sb("g12", [P, TT, 2])
        oh = sb("oh", [P, 2, TT, E])
        msk = sb("msk", [P, TT, E])
        rank = sb("rank", [P, TT, RC])
        gate = sb("gate", [P, TT, RC])
        counts = sb("counts", [P, E + 1], I32)
        gate_slot = sb("gate_slot", [P, 1])
        largest = sb("largest", [P, 1])

        ident, upper, ones, iota = (cst[:, P * i:P * (i + 1)] for i in range(4))
        gnorm_row = sb("gnorm_row", [P, P])
        diag = sb("diag", [P, DIAGS, P])

        prod = xs[:, :, :].rearrange("p t (i n) -> p (t i) n", n=T)
        dec = [xs[:, 0, :], xs[:, 1, :]]
        vec_rows = work[0:NV, 0:D]
        mask_rows = work[:, 2048:3072]
        k_t = work[:, 0:1024]
        bsum = work[:, 1024:2048]
        v_t = work[:, 2048:3072].rearrange("p (t c) -> p t c", t=TT)
        sc = work[:, 3072:4608].rearrange("p (b h t) -> p b h t", b=3, h=HEADS)
        keep = work[:, 3072:4096]
        ax = work[:, 4608:5120]
        upad = work[:, 5120:5636].rearrange("p (c t) -> p c t", c=2)
        gq = row[:, :].rearrange("p (t c) -> p t c", t=TT)
        yb = work[:, 0:1024].rearrange("p (t c) -> p t c", t=TT)
        osq = work[:, 1024:2048]
        up_s = [work[:, 512 * i:512 * (i + 1)] for i in range(3)]
        up_p = [work[:, 1536 + 512 * i:2048 + 512 * i] for i in range(3)]
        glu = work[:, 0:KD * (T + PAD)].rearrange("p (c t) -> p c t", c=KD)
        dwc = work[:, 2304:4352].rearrange("p (c t) -> p c t", c=KD)
        sg = [work[:, 4352:4864], work[:, 4864:5376]]
        zz = [work[:, 0:512], work[:, 512:1024]]
        xTf = work[:, 0:2048].rearrange("p (c t) -> p c t", c=KD)
        moe_s = [work[:, 0:512], work[:, 512:1024]]
        moe_p = [work[:, 1024:1536], work[:, 1536:2048]]
        selg = work[:, 2048:2304].rearrange("p (t s) -> p t s", t=TT)
        xg_hi, xg_lo = xT_hi[:, 0:D], xT_lo[:, 0:D]
        y_hi, y_lo = xT_hi[:, D:2 * D], xT_lo[:, D:2 * D]

        ps = ctx.enter_context(nc.psum_tensor("ps", [P, 8, 512], F32))

        landed = [sem(f"landed{i}") for i in range(RAW)]
        x_in = [sem(f"x_in{t}") for t in range(TT)]
        cst_in = sem("cst_in")
        vec_in = sem("vec_in")
        masks_in = sem("masks_in")
        gnorm_in = sem("gnorm_in")
        router_in = sem("router_in")
        tile_done = sem("tile_done")
        diag_ready = sem("diag_ready")
        diag_used = sem("diag_used")
        pool_step = sem("pool_step")
        prod_made = sem("prod_made")
        conv_copied = sem("conv_copied")
        row_in = sem("row_in")
        out_done = sem("out_done")
        hi_done = sem("hi_done")
        lo_done = sem("lo_done")
        unit_done = sem("unit_done")
        zeroed = sem("zeroed")
        sq_done = sem("sq_done")
        ms_ready = sem("ms_ready")
        rstd_ready = sem("rstd_ready")
        xs_ready = sem("xs_ready")
        turned = sem("turned")
        xh_done = sem("xh_done")
        xl_done = sem("xl_done")
        vec_turned = sem("vec_turned")
        low_dif = sem("low_dif")
        masks_ready = sem("masks_ready")
        low_exp = sem("low_exp")
        dve_own = sem("dve_own")
        sig_done = sem("sig_done")
        fg_ready = sem("fg_ready")
        ln_done = sem("ln_done")
        k_ready = sem("k_ready")
        q_copied = sem("q_copied")
        e_ready = sem("e_ready")
        summed = sem("summed")
        sc_zeroed = sem("sc_zeroed")
        off_ready = sem("off_ready")
        exp_done = sem("exp_done")
        dec_ready = sem("dec_ready")
        scored = sem("scored")
        masked = sem("masked")
        cross_copied = sem("cross_copied")
        in_copied = sem("in_copied")
        ab_read = sem("ab_read")
        ya_hi = sem("ya_hi")
        ya_lo = sem("ya_lo")
        g_silu = sem("g_silu")
        o_done = sem("o_done")
        o_sq = sem("o_sq")
        o_sum = sem("o_sum")
        o_ms = sem("o_ms")
        o_rstd = sem("o_rstd")
        yb_ready = sem("yb_ready")
        yb_turned = sem("yb_turned")
        yb_hi = sem("yb_hi")
        yb_lo = sem("yb_lo")
        res_added = sem("res_added")
        up_silu = sem("up_silu")
        up_mul = sem("up_mul")
        up_hi = sem("up_hi")
        up_lo = sem("up_lo")
        sg_done = sem("sg_done")
        glu_done = sem("glu_done")
        conv_step = sem("conv_step")
        conv_turned = sem("conv_turned")
        ln_var = sem("ln_var")
        ln_ms = sem("ln_ms")
        ln_rstd = sem("ln_rstd")
        ln_ready = sem("ln_ready")
        ln_turned = sem("ln_turned")
        z_silu = sem("z_silu")
        z_hi = sem("z_hi")
        z_lo = sem("z_lo")
        bias_added = sem("bias_added")
        lgT_done = sem("lgT_done")
        lg_turned = sem("lg_turned")
        weighed = sem("weighed")
        counted = sem("counted")
        logits_done = sem("logits_done")
        gd_ready = sem("gd_ready")
        ge_done = sem("ge_done")
        mask_ready = sem("mask_ready")
        rank_done = sem("rank_done")
        routed = sem("routed")
        most_found = sem("most_found")
        y_half = sem("y_half")
        sel_ready = sem("sel_ready")
        gathered = sem("gathered")
        gath_hi = sem("gath_hi")
        gath_lo = sem("gath_lo")
        moe_ready = sem("moe_ready")
        silu_done = sem("silu_done")
        mul_done = sem("mul_done")
        act_turned = sem("act_turned")
        ah_done = sem("ah_done")
        al_done = sem("al_done")
        selg_turned = sem("selg_turned")
        selT_done = sem("selT_done")
        yh_done = sem("yh_done")
        yl_done = sem("yl_done")
        comb_done = sem("comb_done")
        comb_added = sem("comb_added")
        fin_ready = sem("fin_ready")

        w_in, w_out = ev_w_in[0], ev_w_out[0]
        w1, w3, w2 = ev_ffn_w1[0], ev_ffn_w3[0], ev_ffn_w2[0]
        pw1, pw2 = od_w_pw1[0], od_w_pw2[0]

        def hi_unit(k):
            return w_hi[:, k % SPLIT, :]

        def lo_unit(k):
            return w_lo[:, k % SPLIT, :]

        def split_hi(act, k, turn=0):
            act.wait_ge(landed[k % RAW], 16 * turn + 16 * (k // RAW + 1))
            if k >= SPLIT:
                act.wait_ge(unit_done, RAW * turn + k - SPLIT + 1)
            act.activation(hi_unit(k), raw[:, k % RAW, :], ACT.Copy).then_inc(hi_done, 1)

        def split_lo(dve, k, turn=0):
            dve.wait_ge(hi_done, RAW * turn + k + 1)
            dve.tensor_tensor(lo_unit(k), raw[:, k % RAW, :], hi_unit(k).bitcast(F32),
                              ALU.subtract).then_inc(lo_done, 1)

        def load(sp, k, src, turn=0):
            if k >= RAW:
                sp.wait_ge(lo_done, RAW * turn + k - RAW + 1)
            sp.dma_start(raw[:, k % RAW, :].rearrange("p (r n) -> p r n", r=src.shape[1]),
                         src).then_inc(landed[k % RAW], 16)

        def cols(w, n0, n):
            return w[:, bass.ds(n0, n)].rearrange("(k p) n -> p k n", p=P)

        def rows(w, k0, k):
            return w[k0 * P:(k0 + k) * P, :].rearrange("(k p) n -> p k n", p=P)

        def conv_sum(c):
            return ps[:, (0, 1, 2, 5)[c // 2], 0:T]

        def shared_sum(c):
            return ps[:, (3, 7)[(c - SHARED[0]) // 2], T * (c % 2):T * (c % 2 + 1)]

        def step_of(order, c):
            return order.index((c, OWN_TAPS[c] - 1)) + 1

        def taps_until(c):
            return PE_TAPS.index((c, CONF_K - 1)) + 1

        block = ctx.enter_context(nc.Block())

        @block.sync
        def _(sp):
            for t in range(TT):
                sp.dma_start(h[:, t, :], x[0, t * P:(t + 1) * P, :]).then_inc(x_in[t], 16)
            sp.dma_start(cst[:, :], const_f32).then_inc(cst_in, 16)
            for k in range(N_IN):
                load(sp, k, cols(w_in, IN_COLS[k], 256))
                if k == 0:
                    for r, v in ((V_BDW, od_b_dw), (V_LNG, od_ln_g), (V_LNB, od_ln_b)):
                        sp.dma_start(vec_rows[r:r + 1, :], v[0:1, :]).then_inc(vec_in, 16)
                    sp.dma_start(vec_rows[V_BA:V_BA + 2, :], od_b_pw1.rearrange("a (r c) -> (a r) c", r=2)).then_inc(vec_in, 16)
                    sp.dma_start(vec_rows[V_DW:V_DW + CONF_K, :], od_w_dw[0]).then_inc(vec_in, 16)
                    for a in range(2):
                        at = slice(a * CONV, (a + 1) * CONV)
                        sp.dma_start(vec_rows[V_LOW:V_LOW + 3, at], hgrn_lower_bounds).then_inc(vec_in, 16)
                        sp.dma_start(vec_rows[V_CW:V_CW + TAPS, at], ev_conv_w[0]).then_inc(vec_in, 16)
                if k == 2:
                    sp.dma_start(mask_rows, const_masks).then_inc(masks_in, 16)
                    sp.dma_start(gnorm_row[:, :], ev_gnorm[0:1, :].to_broadcast([P, P])).then_inc(gnorm_in, 16)
                    sp.dma_start(router[:, :, :], od_router[0].rearrange("(k p) e -> p k e", p=P)).then_inc(router_in, 16)
            for j in range(N_OUT):
                load(sp, U_OUT + j, rows(w_out, 2 * j, 2))
            with sp.Fori(0, PAIRS // 3) as i:
                for m in range(3):
                    load(sp, U_UP + 2 * m, cols(w1, i * 768 + 256 * m, 256), i)
                    load(sp, U_UP + 2 * m + 1, cols(w3, i * 768 + 256 * m, 256), i)
            for j in range(PAIRS // 3 * 3, PAIRS):
                load(sp, U_UP + 2 * j, cols(w1, 256 * j, 256))
                load(sp, U_UP + 2 * j + 1, cols(w3, 256 * j, 256))
            for j in range(N_DOWN):
                load(sp, U_DOWN + j, rows(w2, 2 * j, 2))
            for j in range(N_PW1 // 2):
                load(sp, U_PW1 + 2 * j, cols(pw1, 256 * j, 256))
                load(sp, U_PW1 + 2 * j + 1, cols(pw1, D + 256 * j, 256))
            for j in range(N_PW2):
                load(sp, U_PW2 + j, rows(pw2, 2 * j, 2))

            def one(w, e):
                return w[0, bass.ds(e, 1)].rearrange("a k n -> (a k) n")

            def expert_loads(e, p):
                e1, e3, e2 = one(od_moe_w1, e), one(od_moe_w3, e), one(od_moe_w2, e)
                for k in range(PER_PASS):
                    if k < 4 * CHUNKS:
                        src = (e1 if k % 4 < 2 else e3)[k % 2 * 512:k % 2 * 512 + 512, k // 4 * 512:(k // 4 + 1) * 512]
                        src = src.rearrange("(k p) n -> p k n", p=P)
                    else:
                        src = rows(e2, 2 * (k - 4 * CHUNKS), 2)
                    load(sp, DENSE + k, src, TURNS * p)

            with sp.Fori(0, E) as e:
                expert_loads(e, e)
            sp.wait_ge(routed, 1)
            passes = sp.alloc_register("sp_passes")
            sp.reg_mov(passes, E)
            most = sp.value_load(counts[0:1, E:E + 1])
            with sp.If(most > SLOTS):
                with sp.Fori(0, E) as e:
                    n = sp.value_load(counts[0:1, bass.ds(e, 1)])
                    with sp.If(n > SLOTS):
                        expert_loads(e, sp.snap(passes))
                        sp.reg_add(passes, passes, 1)
                    with sp.Else():
                        sp.nop()
                    sp.nop()
                sp.nop()
            with sp.Else():
                sp.nop()
            sp.nop()
            for t in range(TT):
                for half in range(2):
                    at = slice(512 * half, 512 * (half + 1))
                    sp.wait_ge(fin_ready, 2 * t + half + 1)
                    sp.dma_start(out[0, t * P:(t + 1) * P, at], xs[:, t, at]).then_inc(out_done, 16)
            sp.wait_ge(out_done, 16 * 2 * TT)

        @block.gpsimd
        def _(pool):
            def load_row(vec):
                pool.dma_start(row[:, :], vec.to_broadcast([P, D])).then_inc(row_in, 16)

            def norm(n):
                if n:
                    pool.wait_ge(xs_ready, 4 * n)
                for t in range(TT):
                    pool.wait_ge(sq_done, 2 * n + t + 1)
                    pool.tensor_scalar(ms[:, t:t + 1], ss[:, t:t + 1], 1.0 / D, EPS, ALU.mult, ALU.add).then_inc(ms_ready, 1)
                    pool.wait_ge(ms_ready, 2 * n + t + 1)
                    pool.tensor_tensor(rstd[:, t:t + 1], ms[:, t:t + 1], mhalf[:, 0:1], ALU.pow).then_inc(rstd_ready, 1)

            load_row(ev_norm_mix[0:1, :])
            pool.memset(mhalf[:, :], -0.5).then_inc(zeroed, 1)
            pool.wait_ge(zeroed, 1)
            norm(0)
            pool.wait_ge(summed, 1)
            for level in range(1, LEVELS):
                if level >= 2:
                    pool.wait_ge(scored, 2 * (level - 2) + 2)
                b = 1 << (level - 1)
                e4 = dec[level % 2].rearrange("p (n a b) -> p n a b", a=2, b=b)
                s4 = bsum.rearrange("p (n a b) -> p n a b", a=2, b=b)
                end = s4[:, :, 0, b - 1:b].to_broadcast([P, 512 // b, b])
                pool.tensor_tensor(e4[:, :, 0, :], end, s4[:, :, 0, :], ALU.subtract)
                if b < CHUNK:
                    ins = pool.tensor_tensor(e4[:, :, 1, :], s4[:, :, 1, :], end, ALU.subtract)
                else:
                    ins = pool.tensor_copy(e4[:, :, 1, :], s4[:, :, 1, :])
                ins.then_inc(e_ready, 1)
                if level == 1:
                    pool.memset(sc[:, :, :, :], 0.0).then_inc(sc_zeroed, 1)
                    last = bsum.rearrange("p (h c t) -> p h c t", h=HEADS, c=4)[:, :, :, CHUNK - 1]
                    off = cross_off[:, :, :]
                    pool.tensor_tensor(off[:, :, 0:1], last[:, :, 0:1], last[:, :, 1:2], ALU.add)
                    pool.tensor_copy(off[:, :, 1:2], last[:, :, 1:2])
                    pool.memset(off[:, :, 2:3], 0.0)
                    pool.tensor_copy(off[:, :, 3:4], last[:, :, 2:3]).then_inc(off_ready, 1)
            pool.wait_ge(off_ready, 1)
            pool.wait_ge(scored, 2 * (CROSS - 2) + 2)
            e4 = dec[CROSS % 2].rearrange("p (h c t) -> p h c t", h=HEADS, c=4)
            s4 = bsum.rearrange("p (h c t) -> p h c t", h=HEADS, c=4)
            off = cross_off[:, :, :].unsqueeze(3).to_broadcast([P, HEADS, 4, CHUNK])
            pool.tensor_tensor(e4[:, :, 0:2, :], off[:, :, 0:2, :], s4[:, :, 0:2, :], ALU.subtract)
            pool.tensor_tensor(e4[:, :, 2:4, :], s4[:, :, 2:4, :], off[:, :, 2:4, :], ALU.add).then_inc(e_ready, 1)
            pool.wait_ge(o_sum, TT)
            pool.tensor_scalar(osq[:, 0:8], oss[:, :], 1.0 / P, EPS, ALU.mult, ALU.add).then_inc(o_ms, 1)
            pool.wait_ge(o_ms, 1)
            pool.tensor_tensor(orstd[:, :], osq[:, 0:8], mhalf[:, :], ALU.pow).then_inc(o_rstd, 1)
            pool.wait_ge(yb_ready, 2)
            load_row(ev_norm_ffn[0:1, :])
            norm(1)
            pool.wait_ge(xs_ready, 8)
            load_row(od_norm_mix[0:1, :])
            norm(2)
            pool.wait_ge(xs_ready, 12)
            load_row(od_b_pw2[0:1, :])
            for step, (c, tap) in enumerate(POOL_ORDER):
                pool.wait_ge(prod_made, MADE_ORDER.index((c, tap)) + 1)
                if tap > 1:
                    pool.wait_ge(pool_step, POOL_ORDER.index((c, tap - 1)) + 1)
                pool.tensor_tensor(dwc[:, c, :], dwc[:, c, :], prod[:, step % PRODUCTS, :],
                                   ALU.add).then_inc(pool_step, 1)
            pool.wait_ge(ln_var, 1)
            pool.tensor_scalar(ms[:, :], lnmv[:, :, 1], 1.0, EPS, ALU.mult, ALU.add).then_inc(ln_ms, 1)
            pool.wait_ge(ln_ms, 1)
            pool.tensor_tensor(rstd[:, :], ms[:, :], mhalf[:, 0:TT], ALU.pow).then_inc(ln_rstd, 1)
            pool.wait_ge(row_in, 64)
            for t in range(TT):
                pool.tensor_tensor(h[:, t, :], h[:, t, :], row[:, :], ALU.add).then_inc(bias_added, 1)
            pool.wait_ge(bias_added, 2)
            load_row(od_norm_ffn[0:1, :])
            pool.wait_ge(ln_ready, 2)
            norm(3)
            pool.wait_ge(xs_ready, 16)
            load_row(final_norm.unsqueeze(0))
            norm(4)

        @block.scalar
        def _(act):
            def squares(n, p=None):
                for t in range(TT):
                    ready, value = (x_in[t], 16) if n == 0 else (res_added, 4 * (n - 1) + 2 * (t + 1))
                    if n < 4:
                        act.wait_ge(ready, value)
                    else:
                        act.wait_ge(comb_added, 2 * p + 2 + t)
                    act.activation(xs[:, t, :], h[:, t, :], ACT.Square,
                                   accum_out=ss[:, t:t + 1]).then_inc(sq_done, 1)

            def turned_hi(n, b0):
                for j in range(4):
                    act.wait_ge(turned, 4 * n + j + 1)
                    act.activation(xT_hi[:, 512 * j:512 * (j + 1)], ps[:, b0 + j, :], ACT.Copy).then_inc(xh_done, 1)

            def tick(k):
                split_hi(act, k + AHEAD)

            squares(0)
            split_hi(act, 0)
            turned_hi(0, 4)
            split_hi(act, 1)
            for k in range(N_IN):
                tick(k)
                if k == 1:
                    act.wait_ge(low_dif, 1)
                    act.activation(lowe[:, :, :], lowe[:, :, :], ACT.Exp).then_inc(low_exp, 1)
                if k < 2:
                    act.wait_ge(unit_done, k + 1)
                    act.activation(dec[0][:, 512 * k:512 * (k + 1)], ps[:, k, :], ACT.Sigmoid).then_inc(sig_done, 1)
                if k == 2:
                    act.wait_ge(fg_ready, 1)
                    act.activation(dec[1], dec[0], ACT.Ln).then_inc(ln_done, 1)
                if k == 3:
                    act.wait_ge(k_ready, 1)
                    act.wait_ge(ln_done, 1)
                    act.wait_ge(unit_done, 4)
                    act.activation(dec[0].rearrange("p (b n) -> p b n", b=2), ps[:, 2:4, :],
                                   ACT.Copy).then_inc(q_copied, 1)
                if k == 4:
                    act.wait_ge(masks_ready, 1)
                if k in (4, 5, 6, 7):
                    act.wait_ge(unit_done, k + 1)
                    into = (v_t if k < 6 else gq)[:, :, 256 * (k % 2):256 * (k % 2 + 1)]
                    act.activation(into, ps[:, k % 2, :].rearrange("p (t c) -> p t c", t=TT),
                                   ACT.Copy).then_inc(in_copied, 1)
                if k in (8, 11):
                    act.wait_ge(unit_done, k + 1)
                    if k == 11:
                        act.wait_ge(ya_lo, 1)
                    act.activation(ax, ps[:, 0 if k == 8 else 1, :], ACT.Copy).then_inc(in_copied, 1)
                if 4 <= k <= 11:
                    level = k - 3
                    act.wait_ge(e_ready, level)
                    act.activation(dec[level % 2], dec[level % 2], ACT.Exp).then_inc(exp_done, 1)
                if k in (10, 13):
                    half = (k - 10) // 3
                    act.wait_ge(ab_read, half + 1)
                    act.activation(act_hi[:, 512 * half:512 * (half + 1)], ax, ACT.Copy).then_inc(ya_hi, 1)
                if k == 12:
                    act.wait_ge(in_copied, 4)
                    act.activation(row[:, :], row[:, :], ACT.Silu).then_inc(g_silu, 1)
                    act.wait_ge(scored, 2 * LEVELS + 1)
                    act.activation(sc[:, 1, :, :], ps[:, 4, :].rearrange("p (h t) -> p h t", h=HEADS),
                                   ACT.Copy).then_inc(cross_copied, 1)
            for j in range(N_OUT):
                tick(U_OUT + j)
                if j == 0:
                    for t in range(TT):
                        act.wait_ge(o_done, t + 1)
                        act.activation(osq[:, 512 * t:512 * (t + 1)], ps[:, 6 + t, :], ACT.Square).then_inc(o_sq, 1)
                if j == 1:
                    for b in range(2):
                        act.wait_ge(yb_turned, b + 1)
                        act.activation(act_hi[:, D + 512 * b:D + 512 * (b + 1)], ps[:, 4 + b, :],
                                       ACT.Copy).then_inc(yb_hi, 1)
            squares(1)
            turned_hi(1, 4)

            def up_ticks(m, i=0):
                k = U_UP + 2 * m
                split_hi(act, k + AHEAD, i)
                act.wait_ge(unit_done, RAW * i + k + 1)
                act.activation(up_s[m % 3], ps[:, 2 * (m % 3), :], ACT.Silu).then_inc(up_silu, 1)
                split_hi(act, k + 1 + AHEAD, i)
                act.wait_ge(up_mul, 3 * i + m + 1)
                act.activation(act_hi[:, bass.ds(i * 1536 + 512 * m, 512)], up_p[m % 3], ACT.Copy).then_inc(up_hi, 1)

            with act.Fori(0, PAIRS // 3) as i:
                for m in range(3):
                    up_ticks(m, i)
            for m in range(PAIRS // 3 * 3, PAIRS):
                up_ticks(m)
            for j in range(N_DOWN):
                tick(U_DOWN + j)
            squares(2)
            turned_hi(2, 0)

            made = [0]

            def make_products(n):
                for c, tap in MADE_ORDER[made[0]:made[0] + n]:
                    act.wait_ge(glu_done, c + 1)
                    wt = vecT[:, c, V_DW + tap:V_DW + tap + 1]
                    if tap == 0:
                        ins = act.activation(dwc[:, c, :], glu[:, c, 0:T], ACT.Identity, scale=wt,
                                             bias=vecT[:, c, V_BDW:V_BDW + 1])
                    else:
                        step = POOL_ORDER.index((c, tap))
                        if step >= PRODUCTS:
                            act.wait_ge(pool_step, step - PRODUCTS + 1)
                        ins = act.activation(prod[:, step % PRODUCTS, :], glu[:, c, tap:tap + T], ACT.Copy, scale=wt)
                    ins.then_inc(prod_made, 1)
                made[0] += n

            for j in range(N_PW1 // 2):
                tick(U_PW1 + 2 * j)
                if j:
                    make_products(7)
                tick(U_PW1 + 2 * j + 1)
                act.wait_ge(unit_done, U_PW1 + 2 * j + 2)
                if j >= 2:
                    act.wait_ge(glu_done, 2 * (j - 1))
                for m in range(2):
                    c = 2 * j + m
                    act.activation(sg[j % 2][:, T * m:T * (m + 1)], ps[:, 5 + 2 * (j % 2), T * m:T * (m + 1)],
                                   ACT.Sigmoid, bias=vecT[:, c, V_BB:V_BB + 1]).then_inc(sg_done, 1)
                if j < N_PW1 // 2 - 1:
                    make_products(7)
            for n, (c, tap) in enumerate(PE_TAPS):
                if n >= DIAGS:
                    act.wait_ge(diag_used, n - DIAGS + 1)
                act.activation(diag[:, n % DIAGS, :], ident, ACT.Copy,
                               scale=vecT[:, c, V_DW + tap:V_DW + tap + 1]).then_inc(diag_ready, 1)
                if n >= DIAGS and n % 2:
                    make_products(1)
            make_products(len(MADE_ORDER) - made[0])
            for c in range(0, KD, 2):
                if c in SHARED:
                    act.wait_ge(diag_used, taps_until(c + 1))
                else:
                    act.wait_ge(conv_step, step_of(DVE_ORDER, c))
                act.activation(dwc[:, c, :], shared_sum(c) if c in SHARED else conv_sum(c),
                               ACT.Copy).then_inc(conv_copied, 1)
            for j in range(4):
                act.wait_ge(ln_turned, j + 1)
                if j >= 2:
                    act.wait_ge(z_lo, j - 1)
                for m in range(2):
                    c = 2 * j + m
                    act.activation(zz[j % 2][:, T * m:T * (m + 1)], ps[:, j, T * m:T * (m + 1)], ACT.Silu,
                                   bias=vecT[:, c, V_LNB:V_LNB + 1],
                                   scale=vecT[:, c, V_LNG:V_LNG + 1]).then_inc(z_silu, 1)
                act.wait_ge(z_silu, 2 * (j + 1))
                act.activation(act_hi[:, 512 * j:512 * (j + 1)], zz[j % 2], ACT.Copy).then_inc(z_hi, 1)
            for j in range(N_PW2):
                tick(U_PW2 + j)
            squares(3)
            for j in range(4):
                act.wait_ge(turned, 12 + j + 1)
                act.activation(xTf[:, 2 * j:2 * j + 2, :], ps[:, j, :].rearrange("p (c t) -> p c t", c=2),
                               ACT.Copy).then_inc(xh_done, 1)
            act.wait_ge(logits_done, 1)
            act.activation(lgT[:, :], ps[0:E, 4, 0:T], ACT.Copy).then_inc(lgT_done, 1)
            act.wait_ge(gd_ready, 1)
            act.activation(ge[:, :], gd[:, :], ACT.Exp).then_inc(ge_done, 1)

            def gather_hi(n, r):
                act.wait_ge(gathered, 2 * n + r - 1)
                act.activation(xg_hi[:, 512 * r:512 * (r + 1)], ps[:, 5, :], ACT.Copy).then_inc(gath_hi, 1)

            def y_round(p):
                act.wait_ge(unit_done, PER_PASS * p + DENSE)
                act.wait_ge(selT_done, p + 1)
                act.wait_ge(comb_added, 2 * p + 1)
                act.activation(y_hi.rearrange("p (b n) -> p b n", b=2), ps[:, 6:8, :], ACT.Copy,
                               scale=gate_slot[:, 0:1]).then_inc(yh_done, 1)

            def expert_pass(p, own_gather, g_off):
                if own_gather:
                    for k in range(AHEAD):
                        split_hi(act, DENSE + k, TURNS * p)
                y_round(p)
                if own_gather:
                    for r in range(2):
                        gather_hi(p + g_off, r)
                for k in range(PER_PASS):
                    if k + AHEAD < PER_PASS:
                        split_hi(act, DENSE + k + AHEAD, TURNS * p)
                    elif not own_gather:
                        with act.If(p < E - 1):
                            split_hi(act, DENSE + k + AHEAD, TURNS * p)
                        with act.Else():
                            act.nop()
                        act.nop()
                    c = k // 4
                    if k < 4 * CHUNKS and k % 4 == 1:
                        act.wait_ge(unit_done, PER_PASS * p + DENSE + k + 1)
                        act.wait_ge(mul_done, CHUNKS * p + (c if c >= 2 else 1))
                        act.activation(moe_s[c % 2], ps[:, 2 * (c % 2), :], ACT.Silu).then_inc(silu_done, 1)
                    if k % 4 == 1 and 1 <= c <= CHUNKS:
                        act.wait_ge(act_turned, CHUNKS * p + c + 1)
                        act.activation(act_hi[:, 512 * (c - 1):512 * c], ps[:, 4, :], ACT.Copy).then_inc(ah_done, 1)
                    if not own_gather and k in (31, 35):
                        gather_hi(p + g_off + 1, (k - 31) // 4)

            for r in range(2):
                gather_hi(1, r)
            act.wait_ge(moe_ready, 1)
            with act.Fori(0, E) as e:
                expert_pass(e, False, 1)
            act.wait_ge(routed, 1)
            passes = act.alloc_register("act_passes")
            act.reg_mov(passes, E)
            most = act.value_load(counts[0:1, E:E + 1])
            with act.If(most > SLOTS):
                with act.Fori(0, E) as e:
                    n = act.value_load(counts[0:1, bass.ds(e, 1)])
                    with act.If(n > SLOTS):
                        expert_pass(act.snap(passes), True, 2)
                        act.reg_add(passes, passes, 1)
                    with act.Else():
                        act.nop()
                    act.nop()
                act.nop()
            with act.Else():
                act.nop()
            act.nop()
            p = act.snap(passes)
            act.wait_ge(selT_done, p + 1)
            act.wait_ge(comb_added, 2 * p + 1)
            for half in range(2):
                if half == 0:
                    act.wait_ge(y_half, p)
                else:
                    act.wait_ge(unit_done, PER_PASS * p + DENSE)
                act.activation(y_hi[:, 512 * half:512 * (half + 1)], ps[:, 6 + half, :], ACT.Copy,
                               scale=gate_slot[:, 0:1]).then_inc(yh_done, 1)
            squares(4, p)

        @block.vector
        def _(dve):
            own = [0]

            def link(ins):
                own[0] += 1
                ins.then_inc(dve_own, 1)
                dve.wait_ge(dve_own, own[0])

            def tick(k):
                split_lo(dve, k + AHEAD)

            def norm_rows(n):
                dve.wait_ge(row_in, 16 * (n + 1 + (n >= 3)))
                for t in range(TT):
                    dve.wait_ge(rstd_ready, 2 * n + t + 1)
                    for half in range(2):
                        at = slice(512 * half, 512 * (half + 1))
                        dve.scalar_tensor_tensor(xs[:, t, at], h[:, t, at], rstd[:, t:t + 1], row[:, at],
                                                 ALU.mult, ALU.mult).then_inc(xs_ready if n < 4 else fin_ready, 1)

            def turned_lo(n, b0):
                for j in range(4):
                    dve.wait_ge(xh_done, 4 * n + j + 1)
                    dve.tensor_tensor(xT_lo[:, 512 * j:512 * (j + 1)], ps[:, b0 + j, :],
                                      xT_hi[:, 512 * j:512 * (j + 1)].bitcast(F32), ALU.subtract).then_inc(xl_done, 1)

            def residual(n, banks, last):
                for t in range(TT):
                    dve.wait_ge(*((tile_done, n + 1) if t == 0 else (unit_done, last + 1)))
                    for half in range(2):
                        part = h[:, t, 512 * half:512 * (half + 1)]
                        ins = dve.tensor_tensor(part, part, ps[:, banks + 2 * t + half, :], ALU.add)
                        ins.then_inc(res_added, 1)

            norm_rows(0)
            split_lo(dve, 0)
            turned_lo(0, 4)
            split_lo(dve, 1)
            dve.wait_ge(masks_in, 16)
            dve.tensor_copy(masks[:, :, :], mask_rows.rearrange("p (l t) -> p l t", l=LEVELS)).then_inc(masks_ready, 1)
            dve.wait_ge(vec_turned, 1)
            link(dve.tensor_copy(vecT[:, :, :], ps[:, 7, 0:KD * NV].rearrange("p (k v) -> p k v", k=KD)))
            low = [vecT[:, 0:4, V_LOW + i] for i in range(3)]
            link(dve.tensor_tensor(lowm[:, :], low[0], low[1], ALU.max))
            link(dve.tensor_tensor(lowm[:, :], lowm[:, :], low[2], ALU.max))
            for i in range(3):
                ins = dve.tensor_tensor(lowe[:, i, :], low[i], lowm[:, :], ALU.subtract)
            ins.then_inc(low_dif, 1)
            tick(0)
            dve.wait_ge(low_exp, 1)
            link(dve.tensor_tensor(lows[:, :], lowe[:, 0, :], lowe[:, 1, :], ALU.add))
            link(dve.tensor_tensor(lows[:, :], lows[:, :], lowe[:, 2, :], ALU.add))
            link(dve.reciprocal(lows[:, :], lows[:, :]))
            link(dve.tensor_tensor(lb[:, :], lowe[:, 0, :], lows[:, :], ALU.mult))
            link(dve.tensor_scalar(olb[:, :], lb[:, :], -1.0, 1.0, ALU.mult, ALU.add))
            link(dve.memset(keep, 1.0))
            link(dve.memset(keep.rearrange("p (c t) -> p c t", t=CHUNK)[:, :, 0:1], 0.0))
            link(dve.memset(upad[:, :, 0:TAPS - 1], 0.0))

            def decay(level):
                dve.wait_ge(exp_done, level)
                n, b = (512 // (1 << (level - 1)), 1 << (level - 1)) if level < CROSS else (HEADS, P)
                e4 = dec[level % 2].rearrange("p (n a b) -> p n a b", n=n, a=2)
                k4 = k_t.rearrange("p (n a b) -> p n a b", n=n, a=2)
                q4 = ps[:, 2:4, :].rearrange("p c w -> p (c w)").rearrange("p (n a b) -> p n a b", n=n, a=2)
                dve.tensor_tensor(e4[:, :, 0, :], e4[:, :, 0, :], k4[:, :, 0, :], ALU.mult)
                dve.tensor_tensor(e4[:, :, 1, :], e4[:, :, 1, :], q4[:, :, 1, :], ALU.mult).then_inc(dec_ready, 1)

            def pick(level):
                for t in range(TT):
                    dve.wait_ge(scored, 2 * level + t + 1)
                    dve.copy_predicated(sc[:, 2 * t, :, :], masks[:, level, :].unsqueeze(1).to_broadcast([P, HEADS, P]),
                                        ps[:, 4 + t, :].rearrange("p (h t) -> p h t", h=HEADS)).then_inc(masked, 1)

            def conv_half(half):
                a2 = ax.rearrange("p (c t) -> p c t", c=2)
                dve.wait_ge(in_copied, 5 + half)
                dve.wait_ge(unit_done, 10 + 3 * half)
                own[0] += 1
                dve.tensor_tensor(upad[:, :, TAPS - 1:], ps[:, 1 - half, :].rearrange("p (c t) -> p c t", c=2), a2,
                                  ALU.mult).then_inc(dve_own, 1)
                dve.wait_ge(dve_own, own[0])
                for tap in range(TAPS):
                    for c in range(2):
                        wt = vecT[:, 2 * half + c, V_CW + tap:V_CW + tap + 1]
                        if tap == 0:
                            ins = dve.tensor_scalar(a2[:, c, :], upad[:, c, 0:T], wt, None, ALU.mult)
                        else:
                            ins = dve.scalar_tensor_tensor(a2[:, c, :], upad[:, c, tap:tap + T], wt, a2[:, c, :],
                                                           ALU.mult, ALU.add)
                        if c:
                            link(ins)

            def gate_half(half):
                dve.wait_ge(unit_done, 11 + 3 * half)
                dve.tensor_tensor(ax, ax, ps[:, half, :], ALU.mult).then_inc(ab_read, 1)
                dve.wait_ge(ya_hi, half + 1)
                dve.tensor_tensor(act_lo[:, 512 * half:512 * (half + 1)], ax,
                                  act_hi[:, 512 * half:512 * (half + 1)].bitcast(F32), ALU.subtract).then_inc(ya_lo, 1)

            for k in range(N_IN):
                if k:
                    tick(k)
                if k == 1:
                    dve.wait_ge(sig_done, 2)
                    for hd in range(HEADS):
                        part = dec[0][:, T * hd:T * (hd + 1)]
                        ins = dve.tensor_scalar(part, part, olb[:, hd:hd + 1], lb[:, hd:hd + 1], ALU.mult, ALU.add)
                    ins.then_inc(fg_ready, 1)
                    dve.wait_ge(fg_ready, 1)
                    dve.tensor_scalar(k_t, dec[0], -1.0, 1.0, ALU.mult, ALU.add).then_inc(k_ready, 1)
                if k == 2:
                    dve.wait_ge(ln_done, 1)
                    dve.tensor_tensor_scan(bsum, keep, dec[1], 0.0, ALU.mult, ALU.add).then_inc(summed, 1)
                if 4 <= k <= 11:
                    decay(k - 3)
                    if k == 4:
                        dve.wait_ge(sc_zeroed, 1)
                    pick(k - 4)
                if k == 9 or k == 12:
                    conv_half((k - 9) // 3)
                if k == 10 or k == 13:
                    gate_half((k - 10) // 3)
                if k == 12:
                    dve.wait_ge(gnorm_in, 16)
                    dve.wait_ge(g_silu, 1)
                    link(dve.tensor_tensor(row[:, :].rearrange("p (g c) -> p g c", c=P),
                                           row[:, :].rearrange("p (g c) -> p g c", c=P),
                                           gnorm_row[:, :].unsqueeze(1).to_broadcast([P, 8, P]), ALU.mult))
            for j in range(N_OUT - 1):
                tick(U_OUT + j)
                if j == 0:
                    for t in range(TT):
                        dve.wait_ge(o_sq, t + 1)
                        dve.reduce_sum(oss[:, HEADS * t:HEADS * (t + 1)],
                                       osq[:, 512 * t:512 * (t + 1)].rearrange("p (h c) -> p h c", h=HEADS),
                                       AX.X).then_inc(o_sum, 1)
                    dve.wait_ge(o_rstd, 1)
                    for t in range(TT):
                        for hd in range(HEADS):
                            part = slice(P * hd, P * (hd + 1))
                            ins = dve.scalar_tensor_tensor(yb[:, t, part], ps[:, 6 + t, part],
                                                           orstd[:, HEADS * t + hd:HEADS * t + hd + 1],
                                                           gq[:, t, part], ALU.mult, ALU.mult)
                        ins.then_inc(yb_ready, 1)
                if j == 1:
                    for b in range(2):
                        dve.wait_ge(yb_hi, b + 1)
                        dve.tensor_tensor(act_lo[:, D + 512 * b:D + 512 * (b + 1)], ps[:, 4 + b, :],
                                          act_hi[:, D + 512 * b:D + 512 * (b + 1)].bitcast(F32),
                                          ALU.subtract).then_inc(yb_lo, 1)
            residual(0, 0, U_UP - 1)
            norm_rows(1)
            turned_lo(1, 4)
            tick(U_UP - 1)

            def up_ticks(m, i=0):
                k = U_UP + 2 * m
                split_lo(dve, k + AHEAD, i)
                split_lo(dve, k + 1 + AHEAD, i)
                dve.wait_ge(unit_done, RAW * i + k + 2)
                dve.wait_ge(up_silu, 3 * i + m + 1)
                dve.tensor_tensor(up_p[m % 3], up_s[m % 3], ps[:, 2 * (m % 3) + 1, :], ALU.mult).then_inc(up_mul, 1)
                dve.wait_ge(up_hi, 3 * i + m + 1)
                dve.tensor_tensor(act_lo[:, bass.ds(i * 1536 + 512 * m, 512)], up_p[m % 3],
                                  act_hi[:, bass.ds(i * 1536 + 512 * m, 512)].bitcast(F32),
                                  ALU.subtract).then_inc(up_lo, 1)

            with dve.Fori(0, PAIRS // 3) as i:
                for m in range(3):
                    up_ticks(m, i)
            for m in range(PAIRS // 3 * 3, PAIRS):
                up_ticks(m)
            for j in range(N_DOWN - 1):
                tick(U_DOWN + j)
            residual(1, 4, U_PW1 - 1)
            norm_rows(2)
            dve.memset(glu[:, :, 0:PAD], 0.0)
            turned_lo(2, 0)
            tick(U_PW1 - 1)

            def conv_taps(start, n=None):
                for c, tap in DVE_ORDER[start:None if n is None else start + n]:
                    wt = vecT[:, c, V_DW + tap:V_DW + tap + 1]
                    if tap == 0:
                        ins = dve.tensor_scalar(conv_sum(c), glu[:, c, 0:T], wt, vecT[:, c, V_BDW:V_BDW + 1],
                                                ALU.mult, ALU.add)
                    else:
                        dve.wait_ge(conv_step, DVE_ORDER.index((c, tap - 1)) + 1)
                        ins = dve.scalar_tensor_tensor(conv_sum(c), glu[:, c, tap:tap + T], wt, conv_sum(c),
                                                       ALU.mult, ALU.add)
                    ins.then_inc(conv_step, 1)

            for j in range(N_PW1 // 2):
                tick(U_PW1 + 2 * j)
                if j:
                    conv_taps(18 * j - 9, 9)
                tick(U_PW1 + 2 * j + 1)
                dve.wait_ge(sg_done, 2 * (j + 1))
                for m in range(2):
                    c = 2 * j + m
                    dve.scalar_tensor_tensor(glu[:, c, PAD:], ps[:, 4 + 2 * (j % 2), T * m:T * (m + 1)],
                                             vecT[:, c, V_BA:V_BA + 1], sg[j % 2][:, T * m:T * (m + 1)],
                                             ALU.add, ALU.mult).then_inc(glu_done, 1)
                dve.wait_ge(glu_done, 2 * (j + 1))
                conv_taps(18 * j, 9)
            conv_taps(18 * j + 9)
            for c in SHARED:
                dve.wait_ge(conv_copied, c // 2 + 1)
                if c % 2:
                    dve.wait_ge(prod_made, MADE_ORDER.index((c, 0)) + 1)
                    if OWN_TAPS[c] > 1:
                        dve.wait_ge(pool_step, step_of(POOL_ORDER, c))
                else:
                    dve.wait_ge(conv_step, step_of(DVE_ORDER, c))
                dve.tensor_tensor(dwc[:, c, :], dwc[:, c, :], shared_sum(c) if c % 2 else conv_sum(c),
                                  ALU.add).then_inc(conv_step, 1)
            for half in range(2):
                for t in range(TT):
                    dve.wait_ge(conv_turned, 2 * half + t + 1)
                    ins = dve.bn_stats(lnst[:, t, half, :], ps[:, 4 + 2 * t + half, :])
            link(ins)
            for t in range(TT):
                ins = dve.bn_aggr(lnmv[:, t, :], lnst[:, t, :, :].rearrange("p a b -> p (a b)"))
            ins.then_inc(ln_var, 1)
            dve.wait_ge(ln_rstd, 1)
            for t in range(TT):
                dve.tensor_scalar(xs[:, t, :].rearrange("p (b n) -> p b n", b=2), ps[:, 4 + 2 * t:6 + 2 * t, :],
                                  lnmv[:, t, 0:1], rstd[:, t:t + 1],
                                  ALU.subtract, ALU.mult).then_inc(ln_ready, 1)
            for j in range(4):
                dve.wait_ge(z_hi, j + 1)
                dve.tensor_tensor(act_lo[:, 512 * j:512 * (j + 1)], zz[j % 2],
                                  act_hi[:, 512 * j:512 * (j + 1)].bitcast(F32), ALU.subtract).then_inc(z_lo, 1)
            for j in range(N_PW2 - 1):
                tick(U_PW2 + j)
            dve.wait_ge(bias_added, 2)
            residual(2, 4, DENSE - 1)
            norm_rows(3)
            dve.memset(ps[:, 6:8, :], 0.0).then_inc(moe_ready, 1)
            dve.memset(gate_slot[:, :], 0.0).then_inc(comb_added, 1)
            dve.memset(gate[:, :, E:E + 1], 0.0).then_inc(mul_done, 1)
            dve.memset(rank[:, :, E:E + 1], -1.0).then_inc(al_done, 1)
            dve.memset(selT[:, :].bitcast(F32), 0.0).then_inc(selT_done, 1)
            tick(DENSE - 1)
            dve.wait_ge(lg_turned, 1)
            link(dve.tensor_copy(lg[:, :, :], ps[:, 5, 0:TT * E].rearrange("p (t e) -> p t e", t=TT)))
            for t in range(TT):
                ins = dve.max(top[:, t, :], lg[:, t, :])
            link(ins)
            for t in range(TT):
                ins = dve.max_index(topi[:, t, :], top[:, t, :], lg[:, t, :])
            dve.tensor_tensor(gd[:, :].unsqueeze(2), top[:, :, 1:2], top[:, :, 0:1], ALU.subtract).then_inc(gd_ready, 1)
            link(ins)
            link(dve.tensor_copy(topf[:, :, :], topi[:, :, 0:2]))
            for i in range(2):
                for t in range(TT):
                    ins = dve.tensor_scalar(oh[:, i, t, :], iota[:, 0:E], topf[:, t, i:i + 1], None, ALU.is_equal)
            link(ins)
            dve.tensor_tensor(msk[:, :, :], oh[:, 0, :, :], oh[:, 1, :, :], ALU.add).then_inc(mask_ready, 1)
            dve.wait_ge(ge_done, 1)
            link(dve.tensor_scalar(gd[:, :], ge[:, :], 1.0, None, ALU.add))
            link(dve.reciprocal(g12[:, :, 0], gd[:, :]))
            link(dve.tensor_tensor(g12[:, :, 1], ge[:, :], g12[:, :, 0], ALU.mult))
            dve.wait_ge(rank_done, 1)
            dve.wait_ge(mask_ready, 1)
            ranks = ps[:, 4, 0:TT * E].rearrange("p (t e) -> p t e", t=TT)
            for t in range(TT):
                ins = dve.scalar_tensor_tensor(rank[:, t, 0:E], ranks[:, t, :], 1.0, msk[:, t, :], ALU.add, ALU.mult)
            link(ins)
            link(dve.tensor_scalar(rank[:, :, 0:E], rank[:, :, 0:E], -1.0, None, ALU.add))

            def select(col):
                for t in range(TT):
                    ins = dve.tensor_scalar(sel[:, t, :], iota, rank[:, t, bass.ds(col, 1)], None, ALU.is_equal)
                ins.then_inc(sel_ready, 1)

            def weigh(col):
                for t in range(TT):
                    ins = dve.tensor_scalar(selg[:, t, :], iota, rank[:, t, bass.ds(col, 1)],
                                            gate[:, t, bass.ds(col, 1)], ALU.is_equal, ALU.mult)
                ins.then_inc(weighed, 1)

            def gather_lo(n, r):
                dve.wait_ge(gath_hi, 2 * n + r - 1)
                dve.tensor_tensor(xg_lo[:, 512 * r:512 * (r + 1)], ps[:, 5, :],
                                  xg_hi[:, 512 * r:512 * (r + 1)].bitcast(F32), ALU.subtract).then_inc(gath_lo, 1)

            def y_rest(p):
                dve.wait_ge(yh_done, p + 1)
                dve.scalar_tensor_tensor(y_lo.rearrange("p (b n) -> p b n", b=2), ps[:, 6:8, :], gate_slot[:, 0:1],
                                         y_hi.rearrange("p (b n) -> p b n", b=2).bitcast(F32),
                                         ALU.mult, ALU.subtract).then_inc(yl_done, 1)

            def add_combined(p, t):
                dve.wait_ge(comb_done, 2 * p + t + 1)
                for half in range(2):
                    part = h[:, t, 512 * half:512 * (half + 1)]
                    ins = dve.tensor_tensor(part, part, ps[:, 5 - half, :], ALU.add)
                ins.then_inc(comb_added, 1)

            def expert_pass(p, e, own_gather, g_off):
                if own_gather:
                    for k in range(AHEAD):
                        split_lo(dve, DENSE + k, TURNS * p)
                y_rest(p)
                if own_gather:
                    select(e)
                    weigh(e)
                    for r in range(2):
                        gather_lo(p + g_off, r)
                for k in range(PER_PASS):
                    if k + AHEAD < PER_PASS:
                        split_lo(dve, DENSE + k + AHEAD, TURNS * p)
                    elif not own_gather:
                        with dve.If(p < E - 1):
                            split_lo(dve, DENSE + k + AHEAD, TURNS * p)
                        with dve.Else():
                            dve.nop()
                        dve.nop()
                    c = k // 4
                    if k % 4 == 1 and 1 <= c <= CHUNKS:
                        dve.wait_ge(ah_done, CHUNKS * p + c)
                        dve.tensor_tensor(act_lo[:, 512 * (c - 1):512 * c], ps[:, 4, :],
                                          act_hi[:, 512 * (c - 1):512 * c].bitcast(F32), ALU.subtract).then_inc(al_done, 1)
                    if k < 4 * CHUNKS and k % 4 == 3:
                        dve.wait_ge(unit_done, PER_PASS * p + DENSE + k + 1)
                        dve.wait_ge(silu_done, CHUNKS * p + c + 1)
                        dve.wait_ge(act_turned, CHUNKS * p + (c if c >= 2 else 1))
                        dve.tensor_tensor(moe_p[c % 2], moe_s[c % 2], ps[:, 2 * (c % 2) + 1, :],
                                          ALU.mult).then_inc(mul_done, 1)
                    if k == 4:
                        add_combined(p, 0)
                    if k == 8:
                        add_combined(p, 1)
                    if k == 16:
                        dve.wait_ge(selg_turned, p + 1)
                        dve.reduce_sum(gate_slot[:, :], ps[:, 5, 0:T], AX.X)
                        dve.tensor_scalar(selT[:, :], ps[:, 5, 0:T], 0.0, None, ALU.is_gt).then_inc(selT_done, 1)
                    if not own_gather and k == 20:
                        select(e + 1)
                        weigh(e + 1)
                    if not own_gather and k in (31, 35):
                        gather_lo(p + g_off + 1, (k - 31) // 4)

            select(0)
            for t in range(TT):
                ins = dve.tensor_scalar(gate[:, t, 0:E], oh[:, 0, t, :], g12[:, t, 0:1], None, ALU.mult)
            link(ins)
            for t in range(TT):
                ins = dve.scalar_tensor_tensor(gate[:, t, 0:E], oh[:, 1, t, :], g12[:, t, 1:2], gate[:, t, 0:E],
                                               ALU.mult, ALU.add)
            link(ins)
            dve.tensor_copy(gate[:, :, E + 1:RC], gate[:, :, 0:E])
            weigh(0)
            link(dve.tensor_scalar(rank[:, :, E + 1:RC], rank[:, :, 0:E], float(-SLOTS), None, ALU.add))
            dve.wait_ge(counted, 1)
            dve.reduce_max(largest[:, :], ps[:, 4, TT * E:(TT + 1) * E], AX.X).then_inc(most_found, 1)
            dve.wait_ge(most_found, 1)
            dve.tensor_copy(counts[:, E:E + 1], largest[:, :])
            dve.tensor_copy(counts[:, 0:E], ps[:, 4, TT * E:(TT + 1) * E]).then_inc(routed, 1)
            for r in range(2):
                gather_lo(1, r)
            with dve.Fori(0, E) as e:
                expert_pass(e, e, False, 1)
            passes = dve.alloc_register("dve_passes")
            dve.reg_mov(passes, E)
            dve.wait_ge(routed, 1)
            most = dve.value_load(counts[0:1, E:E + 1])
            with dve.If(most > SLOTS):
                with dve.Fori(0, E) as e:
                    n = dve.value_load(counts[0:1, bass.ds(e, 1)])
                    with dve.If(n > SLOTS):
                        expert_pass(dve.snap(passes), e + (E + 1), True, 2)
                        dve.reg_add(passes, passes, 1)
                    with dve.Else():
                        dve.nop()
                    dve.nop()
                dve.nop()
            with dve.Else():
                dve.nop()
            dve.nop()
            p = dve.snap(passes)
            for half in range(2):
                at = slice(512 * half, 512 * (half + 1))
                dve.wait_ge(yh_done, p + 1 + half)
                dve.scalar_tensor_tensor(y_lo[:, at], ps[:, 6 + half, :], gate_slot[:, 0:1], y_hi[:, at].bitcast(F32),
                                         ALU.mult, ALU.subtract).then_inc(yl_done, 1)
            for t in range(TT):
                for half in range(2):
                    part = h[:, t, 512 * half:512 * (half + 1)]
                    dve.wait_ge(comb_done, 2 * p + 3 + t)
                    ins = dve.tensor_tensor(part, part, ps[:, 2 * t + half, :], ALU.add)
                ins.then_inc(comb_added, 1)
            norm_rows(4)

        @block.tensor
        def _(pe):
            def three(into, a_hi, a_lo, b_hi, b_lo, start, stop):
                pe.matmul(into, a_hi, b_hi, start=start, stop=False)
                pe.matmul(into, a_hi, b_lo, start=False, stop=False)
                return pe.matmul(into, a_lo, b_hi, start=False, stop=stop)

            def by_channel(k, bank, turn=0, fresh=None):
                pe.wait_ge(lo_done, RAW * turn + k + 1)
                for m in range(2):
                    for c in range(KD):
                        if fresh is not None and m == 0 and c % 2 == 0:
                            pe.wait_ge(xl_done, 4 * fresh + c // 2 + 1)
                        at = slice(256 * c + P * m, 256 * c + P * (m + 1))
                        ins = three(ps[:, bank, T * m:T * (m + 1)], hi_unit(k)[:, at], lo_unit(k)[:, at],
                                    xT_hi[:, T * c:T * (c + 1)], xT_lo[:, T * c:T * (c + 1)], c == 0, c == KD - 1)
                ins.then_inc(unit_done, 1)

            def by_token(k, bank):
                pe.wait_ge(lo_done, k + 1)
                for t in range(TT):
                    for c in range(KD):
                        at = slice(T * c + P * t, T * c + P * (t + 1))
                        wt = slice(256 * c, 256 * (c + 1))
                        ins = three(ps[:, bank, 256 * t:256 * (t + 1)], xT_hi[:, at], xT_lo[:, at],
                                    hi_unit(k)[:, wt], lo_unit(k)[:, wt], c == 0, c == KD - 1)
                ins.then_inc(unit_done, 1)

            def to_stream(k, j, n, banks):
                pe.wait_ge(lo_done, k + 1)
                pairs = [(r, t) for r in range(2) for t in range(TT)]
                if j == n - 1:
                    pairs.sort(key=lambda rt: rt[1])
                for r, t in pairs:
                    at = slice(T * (2 * j + r) + P * t, T * (2 * j + r) + P * (t + 1))
                    for half in range(2):
                        wt = slice(D * r + 512 * half, D * r + 512 * (half + 1))
                        ins = three(ps[:, banks + 2 * t + half, :], act_hi[:, at], act_lo[:, at],
                                    hi_unit(k)[:, wt], lo_unit(k)[:, wt], j == 0 and r == 0, j == n - 1 and r == 1)
                    if j == n - 1 and (r, t) == (1, 0):
                        ins.then_inc(tile_done, 1)
                ins.then_inc(unit_done, 1)

            def turn_stream(n, b0):
                for t in range(TT):
                    for c in range(KD):
                        if c % 4 == 0:
                            pe.wait_ge(xs_ready, 4 * n + 2 * t + c // 4 + 1)
                        ins = pe.transpose(ps[:, b0 + c // 2, T * (c % 2) + P * t:T * (c % 2) + P * (t + 1)],
                                           xs[:, t, P * c:P * (c + 1)], ident)
                        if t == TT - 1 and c % 2:
                            ins.then_inc(turned, 1)

            def score(level):
                if level == 0:
                    pe.wait_ge(q_copied, 1)
                    pe.wait_ge(k_ready, 1)
                else:
                    pe.wait_ge(dec_ready, level)
                a = k_t if level == 0 else dec[level % 2]
                b = dec[level % 2]
                for t in range(TT):
                    if level:
                        pe.wait_ge(masked, 2 * (level - 1) + t + 1)
                    for hd in range(HEADS):
                        at = slice(T * hd + P * t, T * hd + P * (t + 1))
                        ins = pe.matmul(ps[:, 4 + t, P * hd:P * (hd + 1)], a[:, at], b[:, at], start=True, stop=True)
                    ins.then_inc(scored, 1)

            pe.wait_ge(cst_in, 16)
            turn_stream(0, 4)
            banks = [0, 1, 2, 3, 0, 1, 0, 1, 0, 1, 0, 1, 0, 1]
            for k in range(N_IN):
                if k in (4, 5):
                    pe.wait_ge(sig_done, k - 3)
                if k in (6, 7, 8, 9):
                    pe.wait_ge(in_copied, k - 5)
                if k == 10:
                    pe.wait_ge(in_copied, 5)
                if k == 11:
                    pe.wait_ge(ab_read, 1)
                if k == 12:
                    pe.wait_ge(ab_read, 1)
                if k == 13:
                    pe.wait_ge(in_copied, 6)
                if k in (4, 5, 6, 7):
                    by_token(k, banks[k])
                else:
                    by_channel(k, banks[k], 0, 0 if k == 0 else None)
                if k == 0:
                    pe.wait_ge(vec_in, 16 * 9)
                    for c in range(KD):
                        ins = pe.transpose(ps[:, 7, NV * c:NV * (c + 1)], vec_rows[:, P * c:P * (c + 1)], ident[0:NV, 0:NV])
                    ins.then_inc(vec_turned, 1)
                if 4 <= k <= 11:
                    score(k - 4)
                if k == 12:
                    pe.wait_ge(dec_ready, CROSS)
                    pe.wait_ge(masked, 2 * LEVELS)
                    for hd in range(HEADS):
                        ins = pe.matmul(ps[:, 4, P * hd:P * (hd + 1)], dec[0][:, T * hd:T * hd + P],
                                        dec[0][:, T * hd + P:T * (hd + 1)], start=True, stop=True)
                    ins.then_inc(scored, 1)
            pe.wait_ge(cross_copied, 1)
            for hd in range(HEADS):
                at = slice(P * hd, P * (hd + 1))
                ins = pe.matmul(ps[:, 6, at], sc[:, 0, hd, :], v_t[:, 0, at], start=True, stop=True)
            ins.then_inc(o_done, 1)
            for hd in range(HEADS):
                at = slice(P * hd, P * (hd + 1))
                pe.matmul(ps[:, 7, at], sc[:, 1, hd, :], v_t[:, 0, at], start=True, stop=False)
                ins = pe.matmul(ps[:, 7, at], sc[:, 2, hd, :], v_t[:, 1, at], start=False, stop=True)
            ins.then_inc(o_done, 1)
            pe.wait_ge(ya_lo, 2)
            to_stream(U_OUT, 0, N_OUT, 0)
            to_stream(U_OUT + 1, 1, N_OUT, 0)
            for t in range(TT):
                pe.wait_ge(yb_ready, t + 1)
                for hd in range(HEADS):
                    ins = pe.transpose(ps[:, 4 + hd // 2, T * (hd % 2) + P * t:T * (hd % 2) + P * (t + 1)],
                                       yb[:, t, P * hd:P * (hd + 1)], ident)
                    if t == TT - 1 and hd % 2:
                        ins.then_inc(yb_turned, 1)
            for b in range(2):
                pe.wait_ge(yb_lo, b + 1)
                to_stream(U_OUT + 2 + b, 2 + b, N_OUT, 0)
            turn_stream(1, 4)

            def up_pair(m, i=0, first=False):
                if not first:
                    pe.wait_ge(up_mul, 3 * i + m - 2)
                by_channel(U_UP + 2 * m, 2 * (m % 3), i, 1 if first and m == 0 else None)
                by_channel(U_UP + 2 * m + 1, 2 * (m % 3) + 1, i)

            for m in range(3):
                up_pair(m, 0, True)
            with pe.Fori(1, PAIRS // 3) as i:
                for m in range(3):
                    up_pair(m, i)
            for m in range(PAIRS // 3 * 3, PAIRS):
                up_pair(m)
            pe.wait_ge(up_mul, PAIRS - 2)
            for j in range(N_DOWN):
                pe.wait_ge(up_lo, j + 1)
                to_stream(U_DOWN + j, j, N_DOWN, 4)
            turn_stream(2, 0)
            for j in range(N_PW1 // 2):
                if j >= 2:
                    pe.wait_ge(glu_done, 2 * (j - 1))
                by_channel(U_PW1 + 2 * j, 4 + 2 * (j % 2), 0, 2 if j == 0 else None)
                by_channel(U_PW1 + 2 * j + 1, 5 + 2 * (j % 2))
            for n, (c, tap) in enumerate(PE_TAPS):
                first = tap == OWN_TAPS[c]
                if first:
                    pe.wait_ge(glu_done, c + 1)
                pe.wait_ge(diag_ready, n + 1)
                pe.matmul(shared_sum(c), diag[:, n % DIAGS, :], glu[:, c, tap:tap + T],
                          start=first, stop=tap == CONF_K - 1).then_inc(diag_used, 1)
            for half in range(2):
                if half == 0:
                    pe.wait_ge(pool_step, step_of(POOL_ORDER, 3))
                    pe.wait_ge(conv_copied, 2)
                else:
                    pe.wait_ge(conv_step, len(DVE_ORDER) + len(SHARED))
                for t in range(TT):
                    for c in range(4):
                        ins = pe.transpose(ps[:, 4 + 2 * t + half, P * c:P * (c + 1)],
                                           dwc[:, 4 * half + c, P * t:P * (t + 1)], ident)
                    ins.then_inc(conv_turned, 1)
            for t in range(TT):
                pe.wait_ge(ln_ready, t + 1)
                for c in range(KD):
                    ins = pe.transpose(ps[:, c // 2, T * (c % 2) + P * t:T * (c % 2) + P * (t + 1)],
                                       xs[:, t, P * c:P * (c + 1)], ident)
                    if t == TT - 1 and c % 2:
                        ins.then_inc(ln_turned, 1)
            for j in range(N_PW2):
                pe.wait_ge(z_lo, j + 1)
                to_stream(U_PW2 + j, j, N_PW2, 4)
            turn_stream(3, 0)
            pe.wait_ge(res_added, 12)
            pe.wait_ge(router_in, 16)
            for c in range(KD):
                if c % 2 == 0:
                    pe.wait_ge(xh_done, 12 + c // 2 + 1)
                ins = pe.matmul(ps[0:E, 4, 0:T], router[:, c, :], xTf[:, c, :], start=c == 0, stop=c == KD - 1)
            ins.then_inc(logits_done, 1)
            pe.wait_ge(lgT_done, 1)
            for t in range(TT):
                ins = pe.transpose(ps[:, 5, E * t:E * (t + 1)], lgT[:, P * t:P * (t + 1)], ident[0:E, 0:E])
            ins.then_inc(lg_turned, 1)
            pe.wait_ge(mask_ready, 1)
            pe.matmul(ps[:, 4, 0:E], upper, msk[:, 0, :], start=True, stop=True).then_inc(act_turned, 1)
            pe.matmul(ps[:, 4, E:2 * E], ones, msk[:, 0, :], start=True, stop=False)
            pe.matmul(ps[:, 4, E:2 * E], upper, msk[:, 1, :], start=False, stop=True).then_inc(rank_done, 1)
            pe.wait_ge(sel_ready, 1)
            pe.matmul(ps[:, 4, 2 * E:3 * E], ones, msk[:, 0, :], start=True, stop=False)
            pe.matmul(ps[:, 4, 2 * E:3 * E], ones, msk[:, 1, :], start=False, stop=True).then_inc(counted, 1)

            def gather(n, r, ready):
                pe.wait_ge(sel_ready, ready)
                if r:
                    pe.wait_ge(gath_lo, 2 * n - 1)
                for c in range(4):
                    ch = slice(512 * r + P * c, 512 * r + P * (c + 1))
                    for t in range(TT):
                        ins = pe.matmul(ps[:, 5, P * c:P * (c + 1)], xs[:, t, ch], sel[:, t, :],
                                        start=t == 0, stop=t == TT - 1)
                ins.then_inc(gathered, 1)

            def combine(p, t):
                if t == 0:
                    pe.wait_ge(yl_done, p + 1)
                    pe.wait_ge(comb_added, 2 * p + 1)
                    pe.wait_ge(al_done, CHUNKS * p + 1)
                else:
                    pe.wait_ge(comb_added, 2 * p + 2)
                for half in range(2):
                    at = slice(512 * half, 512 * (half + 1))
                    pe.matmul(ps[:, 5 - half, :], selT[:, P * t:P * (t + 1)], y_hi[:, at], start=True, stop=False)
                    ins = pe.matmul(ps[:, 5 - half, :], selT[:, P * t:P * (t + 1)], y_lo[:, at], start=False, stop=True)
                ins.then_inc(comb_done, 1)

            def expert_pass(p, own_gather, g_off):
                if own_gather:
                    pe.wait_ge(selT_done, p + 1)
                    for r in range(2):
                        gather(p + g_off, r, p + g_off)
                pe.wait_ge(gath_lo, 2 * (p + g_off))
                for k in range(PER_PASS):
                    c = k // 4
                    if k < 4 * CHUNKS:
                        if k % 4 == 0:
                            pe.wait_ge(mul_done, CHUNKS * p + (c if c >= 2 else 1))
                        pe.wait_ge(lo_done, PER_PASS * p + DENSE + k + 1)
                        for r in range(4):
                            ch = 4 * (k % 2) + r
                            at = slice(SLOTS * ch, SLOTS * (ch + 1))
                            wt = slice(512 * r, 512 * (r + 1))
                            ins = three(ps[:, 2 * (c % 2) + (k % 4) // 2, :], xg_hi[:, at], xg_lo[:, at],
                                        hi_unit(DENSE + k)[:, wt], lo_unit(DENSE + k)[:, wt], ch == 0, ch == KD - 1)
                        ins.then_inc(unit_done, 1)
                    else:
                        j = k - 4 * CHUNKS
                        if j == 0:
                            pe.wait_ge(yl_done, p + 1)
                        pe.wait_ge(al_done, CHUNKS * p + j // 2 + 2)
                        pe.wait_ge(lo_done, PER_PASS * p + DENSE + k + 1)
                        for half in range(2):
                            for r in range(2):
                                at = slice(SLOTS * (2 * j + r), SLOTS * (2 * j + r + 1))
                                wt = slice(D * r + 512 * half, D * r + 512 * (half + 1))
                                ins = three(ps[:, 6 + half, :], act_hi[:, at], act_lo[:, at],
                                            hi_unit(DENSE + k)[:, wt], lo_unit(DENSE + k)[:, wt],
                                            j == 0 and r == 0, k == PER_PASS - 1 and r == 1)
                            if k == PER_PASS - 1 and half == 0:
                                ins.then_inc(y_half, 1)
                        ins.then_inc(unit_done, 1)
                    if k == 3:
                        combine(p, 0)
                    if k == 7:
                        pe.wait_ge(al_done, CHUNKS * p + 2)
                        combine(p, 1)
                    if k % 4 == 1 and 1 <= c <= CHUNKS:
                        pe.wait_ge(mul_done, CHUNKS * p + c + 1)
                        if c == 1:
                            pe.wait_ge(comb_added, 2 * p + 2)
                        elif c == 2:
                            pe.wait_ge(comb_added, 2 * p + 3)
                        else:
                            pe.wait_ge(al_done, CHUNKS * p + c)
                        for i in range(4):
                            ins = pe.transpose(ps[:, 4, P * i:P * (i + 1)], moe_p[(c - 1) % 2][:, P * i:P * (i + 1)], ident)
                        ins.then_inc(act_turned, 1)
                    if k == 15:
                        pe.wait_ge(weighed, p + g_off)
                        for t in range(TT):
                            ins = pe.transpose(ps[:, 5, P * t:P * (t + 1)], selg[:, t, :], ident)
                        ins.then_inc(selg_turned, 1)
                    if not own_gather and k == 31:
                        pe.wait_ge(selT_done, p + 2)
                        gather(p + g_off + 1, 0, p + g_off + 1)
                    if not own_gather and k == 35:
                        gather(p + g_off + 1, 1, p + g_off + 1)

            for r in range(2):
                gather(1, r, 1)
            with pe.Fori(0, E) as e:
                expert_pass(e, False, 1)
            passes = pe.alloc_register("pe_passes")
            pe.reg_mov(passes, E)
            pe.wait_ge(routed, 1)
            most = pe.value_load(counts[0:1, E:E + 1])
            with pe.If(most > SLOTS):
                with pe.Fori(0, E) as e:
                    n = pe.value_load(counts[0:1, bass.ds(e, 1)])
                    with pe.If(n > SLOTS):
                        expert_pass(pe.snap(passes), True, 2)
                        pe.reg_add(passes, passes, 1)
                    with pe.Else():
                        pe.nop()
                    pe.nop()
                pe.nop()
            with pe.Else():
                pe.nop()
            pe.nop()
            p = pe.snap(passes)
            for half in range(2):
                pe.wait_ge(yl_done, p + 1 + half)
                for t in range(TT):
                    at = slice(512 * half, 512 * (half + 1))
                    pe.matmul(ps[:, 2 * t + half, :], selT[:, P * t:P * (t + 1)], y_hi[:, at], start=True, stop=False)
                    pe.matmul(ps[:, 2 * t + half, :], selT[:, P * t:P * (t + 1)], y_lo[:, at],
                              start=False, stop=True).then_inc(comb_done, 1)


_INS = ['x', 'ev_norm_mix', 'ev_w_in', 'ev_conv_w', 'hgrn_lower_bounds', 'ev_gnorm', 'ev_w_out',
        'ev_norm_ffn', 'ev_ffn_w1', 'ev_ffn_w3', 'ev_ffn_w2', 'od_norm_mix', 'od_w_pw1', 'od_b_pw1',
        'od_w_dw', 'od_b_dw', 'od_ln_g', 'od_ln_b', 'od_w_pw2', 'od_b_pw2', 'od_norm_ffn',
        'od_router', 'od_moe_w1', 'od_moe_w3', 'od_moe_w2', 'final_norm']


def kernel(**inputs):
    import concourse.bacc as bacc
    from concourse.bass_utils import run_bass_kernel_spmd

    nc = bacc.Bacc("TRN2", target_bir_lowering=False, num_devices=1, dynamic_dma_scratch_size=2048)
    arrays = {f"in_{name}": np.ascontiguousarray(inputs[name]) for name in _INS}
    arrays["in_const_f32"], arrays["in_const_masks"] = constants()
    args = [nc.dram_tensor(name, a.shape, mybir.dt.from_np(a.dtype), kind="ExternalInput").ap()
            for name, a in arrays.items()]
    args.append(nc.dram_tensor("out_0", (1, T, D), F32, kind="ExternalOutput").ap())
    build_program(nc, *args)
    r = run_bass_kernel_spmd(nc, [arrays], core_ids=[0])
    return r.results[0]["out_0"]
```
